# Optimizing a Trainium2 kernel written in Bass

```python
import math
import jax, jax.numpy as jnp
from jax import lax
import numpy as np

D_MODEL = 1024
BATCH = 1
SEQ = 256
DEPTH = 2

A_WIDTH = D_MODEL // 2
A_GROUPS = 4
A_GROUP_CH = A_WIDTH // A_GROUPS
A_CHUNK = 128
B_HEAD_DIM = 64
B_HEADS = (D_MODEL // 2) // B_HEAD_DIM
B_WIDTH = B_HEADS * B_HEAD_DIM
MOBA_BLOCK = 256
MOBA_TOPK = 3
MOBA_Q_CHUNK = 8
C_HEAD_DIM = 64
C_HEADS = D_MODEL // C_HEAD_DIM
C_WIDTH = C_HEADS * C_HEAD_DIM
DILATED_CONFIGS = ((128, 1), (512, 4), (2048, 16))
DIL_BLOCK = 128
EVEN_IN = 3 * A_WIDTH + 4 * B_WIDTH
EVEN_MIX = A_WIDTH + B_WIDTH
ODD_IN = 4 * C_WIDTH
N_EVEN = (DEPTH + 1) // 2
N_ODD = DEPTH // 2
NORM_EPS = 1e-6

kernel_name = "hybrid_gmlp_moba_dilated_trunk"

def rms_norm(x, g):
    xf = x.astype(jnp.float32)
    y = xf * lax.rsqrt(jnp.mean(xf * xf, axis=-1, keepdims=True) + NORM_EPS)
    return (y * g.astype(jnp.float32)).astype(x.dtype)

def layer_norm(x, g, b):
    xf = x.astype(jnp.float32)
    mu = jnp.mean(xf, axis=-1, keepdims=True)
    xc = xf - mu
    y = xc * lax.rsqrt(jnp.mean(xc * xc, axis=-1, keepdims=True) + NORM_EPS)
    return (y * g.astype(jnp.float32) + b.astype(jnp.float32)).astype(x.dtype)

def chunked_gmlp(u, v, ln_g, ln_b, w_s, b_s):
    Bn, S, _ = u.shape
    u = jax.nn.gelu(u)
    v = layer_norm(jax.nn.gelu(v), ln_g, ln_b)
    vc = v.reshape(Bn, S // A_CHUNK, A_CHUNK, A_GROUPS, A_GROUP_CH)
    w = jnp.tril(w_s).astype(v.dtype)
    mixed = jnp.einsum('gts,bnsgc->bntgc', w, vc) + b_s.T.astype(v.dtype)[None, None, :, :, None]
    return u * mixed.reshape(Bn, S, A_WIDTH)

def moba_attention(q, k, v):
    Bn, S, H, dh = q.shape
    Sp = -(-S // MOBA_BLOCK) * MOBA_BLOCK
    pad = ((0, 0), (0, Sp - S), (0, 0), (0, 0))
    q, k, v = [jnp.pad(t, pad).transpose(0, 2, 1, 3) for t in (q, k, v)]
    nb = Sp // MOBA_BLOCK
    topk = min(MOBA_TOPK, nb)
    scale = dh ** -0.5
    kb = k.reshape(Bn, H, nb, MOBA_BLOCK, dh)
    vb = v.reshape(Bn, H, nb, MOBA_BLOCK, dh)
    k_mean = jnp.mean(kb.astype(jnp.float32), axis=3)
    gate = jnp.einsum('bhsd,bhnd->bhsn', q.astype(jnp.float32), k_mean)
    pos = jnp.arange(Sp)
    past = jnp.arange(nb)[None, :] < (pos // MOBA_BLOCK)[:, None]
    gate = jnp.where(past[None, None], gate, -jnp.inf)
    top_val, top_idx = lax.top_k(gate, topk)
    sel_valid = jnp.isfinite(top_val)
    flat_idx = (jnp.arange(Bn)[:, None, None, None] * H
                + jnp.arange(H)[None, :, None, None]) * nb + top_idx
    kb_flat = kb.reshape(Bn * H * nb, MOBA_BLOCK, dh)
    vb_flat = vb.reshape(Bn * H * nb, MOBA_BLOCK, dh)
    Tq = MOBA_Q_CHUNK
    n_q = Sp // Tq
    q_ch = q.reshape(Bn, H, n_q, Tq, dh).transpose(2, 0, 1, 3, 4)
    idx_ch = flat_idx.reshape(Bn, H, n_q, Tq, topk).transpose(2, 0, 1, 3, 4)
    val_ch = sel_valid.reshape(Bn, H, n_q, Tq, topk).transpose(2, 0, 1, 3, 4)
    n_sel = topk * MOBA_BLOCK

    def step(args):
        qc, ic, vc_, c = args
        blk = (c * Tq) // MOBA_BLOCK
        k_sel = jnp.take(kb_flat, ic, axis=0)
        v_sel = jnp.take(vb_flat, ic, axis=0)
        k_own = lax.dynamic_slice_in_dim(k, blk * MOBA_BLOCK, MOBA_BLOCK, axis=2)
        v_own = lax.dynamic_slice_in_dim(v, blk * MOBA_BLOCK, MOBA_BLOCK, axis=2)
        l_sel = jnp.einsum('bhqd,bhqnkd->bhqnk', qc, k_sel).astype(jnp.float32) * scale
        l_sel = jnp.where(vc_[..., None], l_sel, -jnp.inf).reshape(Bn, H, Tq, n_sel)
        l_own = jnp.einsum('bhqd,bhkd->bhqk', qc, k_own).astype(jnp.float32) * scale
        qpos = c * Tq + jnp.arange(Tq)
        kpos = blk * MOBA_BLOCK + jnp.arange(MOBA_BLOCK)
        l_own = jnp.where((kpos[None, :] <= qpos[:, None])[None, None], l_own, -jnp.inf)
        p = jax.nn.softmax(jnp.concatenate([l_sel, l_own], axis=-1), axis=-1)
        p_sel = p[..., :n_sel].reshape(Bn, H, Tq, topk, MOBA_BLOCK).astype(v.dtype)
        p_own = p[..., n_sel:].astype(v.dtype)
        return (jnp.einsum('bhqnk,bhqnkd->bhqd', p_sel, v_sel)
                + jnp.einsum('bhqk,bhkd->bhqd', p_own, v_own))

    out = lax.map(step, (q_ch, idx_ch, val_ch, jnp.arange(n_q)))
    out = out.transpose(1, 0, 3, 2, 4).reshape(Bn, Sp, H, dh)
    return out[:, :S]

def dilated_window_attention(q, k, v, window, dil):
    Bn, S, H, dh = q.shape
    n_back = window // dil
    L = DIL_BLOCK
    span = dil * L
    Sp = -(-S // span) * span
    M = Sp // dil
    nb = M // L

    def to_blocks(t):
        t = jnp.pad(t, ((0, 0), (0, Sp - S), (0, 0), (0, 0)))
        return t.reshape(Bn, M, dil, H, dh).transpose(0, 2, 1, 3, 4).reshape(Bn, dil, nb, L, H, dh)

    def with_prev(t):
        prev = jnp.pad(t, ((0, 0), (0, 0), (1, 0), (0, 0), (0, 0), (0, 0)))[:, :, :-1]
        return jnp.concatenate([prev, t], axis=3)

    qb, kb, vb = to_blocks(q), to_blocks(k), to_blocks(v)
    kc, vc = with_prev(kb), with_prev(vb)
    logits = jnp.einsum('brnihd,brnjhd->brnhij', qb, kc).astype(jnp.float32) * (dh ** -0.5)
    i = jnp.arange(L)[:, None]
    j = jnp.arange(2 * L)[None, :]
    rel = L + i - j
    band = (rel >= 0) & (rel <= n_back)
    valid = band[None] & ((jnp.arange(nb)[:, None, None] > 0) | (j >= L)[None])
    logits = jnp.where(valid[None, None, :, None], logits, -jnp.inf)
    m = jnp.max(logits, axis=-1, keepdims=True)
    p = jnp.exp(logits - m)
    den = jnp.sum(p, axis=-1)
    o = jnp.einsum('brnhij,brnjhd->brnihd', p.astype(v.dtype), vc).astype(jnp.float32)
    o = o / den.transpose(0, 1, 2, 4, 3)[..., None]
    lse = (m[..., 0] + jnp.log(den)).transpose(0, 1, 2, 4, 3)
    o = o.reshape(Bn, dil, M, H, dh).transpose(0, 2, 1, 3, 4).reshape(Bn, Sp, H, dh)[:, :S]
    lse = lse.reshape(Bn, dil, M, H).transpose(0, 2, 1, 3).reshape(Bn, Sp, H)[:, :S]
    return o, lse

def dilated_mixture(q, k, v):
    outs, lses = [], []
    for window, dil in DILATED_CONFIGS:
        o, l = dilated_window_attention(q, k, v, window, dil)
        outs.append(o)
        lses.append(l)
    wts = jax.nn.softmax(jnp.stack(lses, axis=0), axis=0)
    y = jnp.einsum('gbsh,gbshd->bshd', wts, jnp.stack(outs, axis=0))
    return y.astype(q.dtype)

def even_layer(hn, w_in, w_out, ln_g, ln_b, w_s, b_s):
    Bn, S, _ = hn.shape
    z = hn @ w_in
    cuts = [A_WIDTH, 2 * A_WIDTH, 3 * A_WIDTH, 3 * A_WIDTH + B_WIDTH,
            3 * A_WIDTH + 2 * B_WIDTH, 3 * A_WIDTH + 3 * B_WIDTH]
    u, v, g_a, q, k, vv, g_b = jnp.split(z, cuts, axis=-1)
    y_a = chunked_gmlp(u, v, ln_g, ln_b, w_s, b_s) * jax.nn.silu(g_a)
    hs = (Bn, S, B_HEADS, B_HEAD_DIM)
    y_b = moba_attention(q.reshape(hs), k.reshape(hs), vv.reshape(hs)).reshape(Bn, S, B_WIDTH)
    y_b = y_b * jax.nn.silu(g_b)
    return jnp.concatenate([y_a, y_b], axis=-1) @ w_out

def odd_layer(hn, w_in, w_out):
    Bn, S, _ = hn.shape
    z = hn @ w_in
    q, k, v, g = jnp.split(z, [C_WIDTH, 2 * C_WIDTH, 3 * C_WIDTH], axis=-1)
    hs = (Bn, S, C_HEADS, C_HEAD_DIM)
    y = dilated_mixture(q.reshape(hs), k.reshape(hs), v.reshape(hs)).reshape(Bn, S, C_WIDTH)
    return (y * jax.nn.silu(g)) @ w_out

def setup_inputs(seed: int = 0) -> dict:
    key = jax.random.key(seed)
    ks = jax.random.split(key, 11)
    f32 = jnp.float32
    nrm = jax.random.normal
    return {
        "x": nrm(ks[0], (BATCH, SEQ, D_MODEL), f32),
        "norm_g": 1.0 + 0.05 * nrm(ks[1], (DEPTH, D_MODEL), f32),
        "final_norm_g": 1.0 + 0.05 * nrm(ks[2], (D_MODEL,), f32),
        "ab_w_in": nrm(ks[3], (N_EVEN, D_MODEL, EVEN_IN), f32) * D_MODEL ** -0.5,
        "ab_w_out": nrm(ks[4], (N_EVEN, EVEN_MIX, D_MODEL), f32) * EVEN_MIX ** -0.5,
        "gmlp_ln_g": 1.0 + 0.05 * nrm(ks[5], (N_EVEN, A_WIDTH), f32),
        "gmlp_ln_b": 0.02 * nrm(ks[6], (N_EVEN, A_WIDTH), f32),
        "gmlp_w_s": nrm(ks[7], (N_EVEN, A_GROUPS, A_CHUNK, A_CHUNK), f32) * A_CHUNK ** -0.5,
        "gmlp_b_s": 1.0 + 0.1 * nrm(ks[8], (N_EVEN, A_GROUPS, A_CHUNK), f32),
        "c_w_in": nrm(ks[9], (N_ODD, D_MODEL, ODD_IN), f32) * D_MODEL ** -0.5,
        "c_w_out": nrm(ks[10], (N_ODD, C_WIDTH, D_MODEL), f32) * C_WIDTH ** -0.5,
    }

def reference(x, norm_g, final_norm_g, ab_w_in, ab_w_out, gmlp_ln_g, gmlp_ln_b,
              gmlp_w_s, gmlp_b_s, c_w_in, c_w_out):
    h = x
    for layer in range(DEPTH):
        idx = layer // 2
        hn = rms_norm(h, norm_g[layer])
        if layer % 2 == 0:
            h = h + even_layer(hn, ab_w_in[idx], ab_w_out[idx], gmlp_ln_g[idx],
                               gmlp_ln_b[idx], gmlp_w_s[idx], gmlp_b_s[idx])
        else:
            h = h + odd_layer(hn, c_w_in[idx], c_w_out[idx])
    return rms_norm(h, final_norm_g)


_drawn_inputs = setup_inputs


def setup_inputs(seed=0):
    import zlib

    import numpy as np

    out = dict(_drawn_inputs(seed))
    spreads = {}
    factors = {'gmlp_ln_g': 6.24, 'gmlp_ln_b': 23.588, 'gmlp_b_s': 3.219}
    for name, (base, spread) in spreads.items():
        noise = np.random.default_rng([zlib.crc32(name.encode()), seed]).standard_normal(out[name].shape)
        drawn = base * np.exp(spread * noise) if base else spread * noise
        out[name] = __import__('jax').numpy.asarray(drawn.astype(out[name].dtype))
    for name, factor in factors.items():
        out[name] = (out[name] * factor).astype(out[name].dtype)
    return out
```

```python
import math
from contextlib import ExitStack

import concourse.bass as bass
from concourse import mybir
from concourse.alu_op_type import AluOpType as ALU

P = 128
SEQ = 256
TILES = SEQ // P
D = 1024
CHUNKS = D // P
BLOCK = 512
HALF_CHUNKS = CHUNKS // 2
HEAD = 64
EVEN_HEADS = 8
ODD_HEADS = 16
GROUPS = 4
EPS = 1e-6
SCALE = HEAD ** -0.5
MASKED = -1e30
GELU_C = math.sqrt(2.0 / math.pi)
GELU_A = 0.044715
RAW_SLOTS = 3
SPLIT_SLOTS = 5


def plan():
    halves, groups, items = [], [], []

    def whole(matrix, column, kind, place):
        g = len(groups)
        groups.append((kind, place))
        for part in range(2):
            h = len(halves)
            halves.append((matrix, part * HALF_CHUNKS, column))
            items.extend((g, h, q, None) for q in range(2))

    def output(matrix, parts):
        g = len(groups)
        groups.extend([("residual", 0), ("residual", 1)])
        for part in parts:
            h = len(halves)
            halves.extend((matrix, part * HALF_CHUNKS, c * BLOCK) for c in range(2))
            for tile in range(TILES):
                items.extend((g + tile, h + c, q, c) for c in range(2) for q in range(2))

    u, v, ga, q, k, vv, gb = (i * BLOCK for i in range(7))
    whole("even_in", q, "query", 0)
    whole("even_in", k, "key", 0)
    whole("even_in", vv, "value", 0)
    whole("even_in", gb, "gate", 1)
    whole("even_in", v, "gelu", 1)
    whole("even_in", u, "gelu", 0)
    whole("even_in", ga, "gate", 0)
    output("even_out", (1, 0))
    g, h = len(groups), len(halves)
    groups.extend([("value_tile", 0), ("value_tile", 1)])
    halves.extend(("odd_in", part * HALF_CHUNKS, 2 * D + c * BLOCK) for c in range(2) for part in range(2))
    for tile in range(TILES):
        items.extend((g + tile, h + i, q, i // 2) for i in range(4) for q in range(2))
    for c in range(2):
        whole("odd_in", c * BLOCK, "query", c)
        whole("odd_in", D + c * BLOCK, "key", c)
    for c in range(2):
        whole("odd_in", 3 * D + c * BLOCK, "gate", c)
    output("odd_out", (0, 1))
    return halves, groups, items


HALVES, GROUPS_OF_BANKS, ITEMS = plan()
LAST_ITEM_OF_GROUP = {item[0]: n for n, item in enumerate(ITEMS)}
LAST_ITEM_OF_HALF = {item[1]: n for n, item in enumerate(ITEMS)}
ACT_KINDS = ("query", "key", "value", "value_tile")


def steps():
    out, split = [], 0
    first_item = {}
    for n, item in enumerate(ITEMS):
        first_item.setdefault(item[0], n)
    extra = {}

    def at(position, *what):
        extra.setdefault(position, []).extend(what)

    def heads(first_position, numbers, pace):
        for n, head in enumerate(numbers):
            p = first_position + pace(n)
            at(p, ("scores", head))
            at(p + 3, ("transpose", head))
            at(p + 5, ("values", head))

    even_attention = 2 * first_item[3]
    heads(even_attention, range(EVEN_HEADS), lambda n: 2 * n)
    ge = 2 * first_item[4] + 8
    at(ge, ("gelu_inner", 4))
    at(ge + 1, ("gelu_outer", 4))
    at(ge + 3, ("layer_norm", 0))
    at(ge + 4, ("layer_norm", 1))
    at(ge + 7, ("mix", 0))
    at(ge + 8, ("gelu_inner", 5))
    at(ge + 9, ("gelu_outer", 5))
    at(ge + 9, ("mix", 1))
    at(ge + 10, ("gating", 0))
    for i in range(4):
        at(ge + 11 + i, ("y_chunk", i))
    at(ge + 15, ("mix_u", 0), ("mix_u", 1))
    out_even = 2 * first_item[7]
    at(out_even + 1, ("gating", 1))
    for i in range(4):
        at(out_even + 3 + 2 * i, ("y_chunk", 4 + i))
    at(2 * first_item[9] - 8, ("residual", 0))
    at(2 * first_item[9] - 5, ("scale", 0))
    at(2 * first_item[9], ("hidden", 2))
    at(2 * first_item[9], ("residual", 1))
    at(2 * first_item[9] + 3, ("scale", 1))
    at(2 * first_item[9] + 8, ("hidden", 3))
    odd_attention = 2 * first_item[13]
    heads(odd_attention, range(EVEN_HEADS, EVEN_HEADS + 8), lambda n: 2 * n)
    heads(2 * first_item[15], range(EVEN_HEADS + 8, EVEN_HEADS + 16), lambda n: n + n // 2)
    g0 = 2 * first_item[16]
    at(g0 + 1, ("gating", 2))
    for i in range(4):
        at(g0 + 2 + 2 * i, ("y_chunk", 8 + i))
    out_odd = 2 * first_item[17]
    at(out_odd + 3, ("gating", 3))
    for i in range(4):
        at(out_odd + 5 + 2 * i, ("y_chunk", 12 + i))

    freed = {}
    for n, item in enumerate(ITEMS):
        for half in range(2):
            while half == 0 and split < 2 * len(HALVES):
                h = split // 2
                needed = min([m for m, i in enumerate(ITEMS) if 2 * i[1] + i[2] == split])
                if needed > n + 6 or (h >= SPLIT_SLOTS and freed.get(h - SPLIT_SLOTS, n) > n - 1):
                    break
                out.append(("split", split))
                split += 1
                if needed > n + 1:
                    break
            out.extend(extra.pop(2 * n + half, ()))
            out.append(("product", n, half))
        for h, last in LAST_ITEM_OF_HALF.items():
            if last == n:
                freed[h] = n
        g = item[0]
        if LAST_ITEM_OF_GROUP[g] == n and GROUPS_OF_BANKS[g][0] not in ("gelu", "residual"):
            out.append(("evacuate", g))
    assert not extra, extra
    out.extend([("residual", 2), ("final", 0), ("residual", 3), ("final", 1)])
    return out


def count_of_kind(kinds, group):
    return sum(k in kinds for k, _ in GROUPS_OF_BANKS[: group + 1])


def build(nc, x, norm_g, final_norm_g, ab_w_in, ab_w_out, gmlp_ln_g, gmlp_ln_b, gmlp_w_s, gmlp_b_s,
          c_w_in, c_w_out, out):
    fp32 = mybir.dt.float32
    fp32r = mybir.dt.float32r
    int32 = mybir.dt.int32
    ACT = mybir.ActivationFunctionType
    matrices = {"even_in": ab_w_in[0], "even_out": ab_w_out[0], "odd_in": c_w_in[0], "odd_out": c_w_out[0]}
    order = steps()
    x_tiles = x[0].rearrange("(t p) c -> t p c", p=P)
    out_tiles = out[0].rearrange("(t p) c -> t p c", p=P)
    N_HEADS = EVEN_HEADS + ODD_HEADS

    ctx = ExitStack()
    with ctx:
        def sb(name, shape, dtype=fp32):
            return ctx.enter_context(nc.sbuf_tensor(name, shape, dtype))

        def sem(name):
            return ctx.enter_context(nc.semaphore(name))

        ctx.enter_context(nc.allow_non_contiguous_dma(reason="a bias of 512 numbers, once"))
        w_raw = sb("w_raw", [P, RAW_SLOTS, HALF_CHUNKS, BLOCK])
        w_hi = sb("w_hi", [P, SPLIT_SLOTS, HALF_CHUNKS, BLOCK], fp32r)
        w_lo = sb("w_lo", [P, SPLIT_SLOTS, HALF_CHUNKS, BLOCK], fp32r)
        h = sb("h", [P, TILES, D])
        hn = sb("hn", [P, TILES, D])
        hnT_hi = sb("hnT_hi", [P, CHUNKS, SEQ], fp32r)
        hnT_lo = sb("hnT_lo", [P, CHUNKS, SEQ], fp32r)
        yT_hi = sb("yT_hi", [P, CHUNKS, SEQ], fp32r)
        yT_lo = sb("yT_lo", [P, CHUNKS, SEQ], fp32r)
        qT = sb("qT", [P, CHUNKS, SEQ])
        kT = sb("kT", [P, CHUNKS, SEQ])
        v = sb("v", [P, TILES, D])
        gate = sb("gate", [P, 2, TILES, BLOCK])
        y = sb("y", [P, TILES, D])
        tanh = sb("tanh", [P, TILES, BLOCK])
        probs = sb("probs", [P, 2, 3 * P])
        probsT = sb("probsT", [P, 2, 3 * P])
        least = sb("least", [P, N_HEADS, 2])
        den = sb("den", [P, N_HEADS, 2])
        rden = sb("rden", [P, N_HEADS, 2])
        mask_even = sb("mask_even", [P, 2 * P])
        mask_odd = sb("mask_odd", [P, 2 * P])
        ident = sb("ident", [P, P])
        bias_s = sb("bias_s", [P, GROUPS])
        sumsq = sb("sumsq", [P, 6])
        rstd = sb("rstd", [P, 8])
        power = sb("power", [P, 1])
        moments = sb("moments", [P, TILES, nc.vector.BN_STATS_DIM])
        meanvar = sb("meanvar", [P, TILES, nc.vector.BN_AGGR_DIM])
        gain = kT[:, 0:4, :].rearrange("p a b -> p (a b)")
        ws = qT[:, 4:6, :].rearrange("p a (b s) -> p (a b) s", s=P)
        wsT = kT[:, 4:6, :].rearrange("p a (b t) -> p (a b) t", t=P)
        ln_g, ln_b = v[:, 0, BLOCK:D], v[:, 1, BLOCK:D]
        rel = probs[:, :, 0:P].bitcast(int32)
        rel4 = gate[:, 0, 0, 0:2 * P].bitcast(int32)
        rel16 = gate[:, 0, 0, 2 * P:4 * P].bitcast(int32)
        rel_i = gate[:, 1, 0, 0:2 * P].bitcast(int32)
        n_held = gate[:, 1, 1, 0:2 * P]
        part_a = gate[:, 0, 1, 0:2 * P]
        part_b = gate[:, 0, 1, 2 * P:4 * P]
        in_window = gate[:, 1, 1, 2 * P:4 * P]

        banks = [ctx.enter_context(nc.psum_tensor(f"products{i}", [P, BLOCK], fp32)) for i in range(4)]
        score_banks = [ctx.enter_context(nc.psum_tensor(f"scores{i}", [P, BLOCK], fp32)) for i in range(2)]
        turn_bank = ctx.enter_context(nc.psum_tensor("turned", [P, BLOCK], fp32))
        value_bank = ctx.enter_context(nc.psum_tensor("attended", [P, BLOCK], fp32))
        free_half = value_bank[:, 2 * P:4 * P]

        w_loaded = [sem(f"w_loaded{i}") for i in range(RAW_SLOTS)]
        x_loaded = [sem(f"x_loaded{i}") for i in range(TILES)]
        gain_loaded = [sem(f"gain_loaded{i}") for i in range(3)]
        ws_loaded, ln_loaded, bias_loaded = sem("ws_loaded"), sem("ln_loaded"), sem("bias_loaded")
        stored = sem("stored")
        hi_ready, lo_ready = sem("hi_ready"), sem("lo_ready")
        products_done = sem("products_done")
        act_emptied, dve_emptied = sem("act_emptied"), sem("dve_emptied")
        const_pool, const_dve = sem("const_pool"), sem("const_dve")
        iota_ready, mask_count = sem("iota_ready"), sem("mask_count")
        mask_built = sem("mask_built")
        ws_masked, ws_turned, wsT_ready = sem("ws_masked"), sem("ws_turned"), sem("wsT_ready")
        squares, rstd_ready, mean_sq = sem("squares"), sem("rstd_ready"), sem("mean_sq")
        added, scaled = sem("added"), sem("scaled")
        hidden_turned, hidden_hi, hidden_ready = sem("hidden_turned"), sem("hidden_hi"), sem("hidden_ready")
        scores_done, masked, probs_ready = sem("scores_done"), sem("masked"), sem("probs_ready")
        probs_turned, probsT_ready = sem("probs_turned"), sem("probsT_ready")
        values_done, inverted, attended = sem("values_done"), sem("inverted"), sem("attended")
        squared, poly, inner_ready = sem("squared"), sem("poly"), sem("inner_ready")
        tanh_ready = sem("tanh_ready")
        stats, stats2, centred, gained, v_normed = (sem("stats"), sem("stats2"), sem("centred"),
                                                    sem("gained"), sem("v_normed"))
        ln_plus = sem("ln_plus")
        mix_done, mixed = sem("mix_done"), sem("mixed")
        gated = sem("gated")
        y_turned, y_hi, y_lo = sem("y_turned"), sem("y_hi"), sem("y_lo")

        def pair(group):
            return banks[2 * (group % 2)], banks[2 * (group % 2) + 1]

        def wait_emptied(engine, group):
            if GROUPS_OF_BANKS[group][0] in ACT_KINDS:
                engine.wait_ge(act_emptied, count_of_kind(ACT_KINDS, group))
            elif GROUPS_OF_BANKS[group][0] == "residual":
                engine.wait_ge(added, count_of_kind(("residual",), group))
            else:
                engine.wait_ge(dve_emptied, count_of_kind(("gate", "gelu"), group))

        def dve_emptied_before(group):
            return count_of_kind(("gate", "gelu"), group - 1)

        def tanh_writes_before(group):
            return TILES * dve_emptied_before(group)

        def head_place(head):
            n = head if head < EVEN_HEADS else head - EVEN_HEADS
            return n // 2, HEAD * (n % 2), HEAD * n

        def y_place(n):
            chunk = (4, 5, 6, 7, 0, 1, 2, 3)[n] if n < CHUNKS else n - CHUNKS
            alone = n in range(8, 12)
            return chunk, (free_half if n % 2 == 0 or alone else turn_bank[:, 0:2 * P]), alone

        block = ctx.enter_context(nc.Block())

        @block.sync
        def _(sp):
            for t in range(TILES):
                sp.dma_start(h[:, t, :], x_tiles[t]).then_inc(x_loaded[t], 16)
            for n, (matrix, chunk, column) in enumerate(HALVES):
                if n >= RAW_SLOTS:
                    sp.wait_ge(lo_ready, 2 * (n - RAW_SLOTS + 1))
                rows = matrices[matrix][chunk * P:(chunk + HALF_CHUNKS) * P, column:column + BLOCK]
                sp.dma_start(w_raw[:, n % RAW_SLOTS], rows.rearrange("(k p) c -> p k c", p=P)
                             ).then_inc(w_loaded[n % RAW_SLOTS], 16)
            for t in range(TILES):
                sp.wait_ge(scaled, 2 * TILES + t + 1)
                sp.dma_start(out_tiles[t], hn[:, t, :]).then_inc(stored, 16)
            sp.wait_ge(stored, 16 * TILES)

        @block.gpsimd
        def _(pool):
            nc.gpsimd.memset(power[:], -0.5)
            nc.gpsimd.memset(ident[:], 0.0)
            nc.gpsimd.memset(mask_even[:], 0.0).then_inc(const_pool, 1)
            pool.wait_ge(const_pool, 1)
            nc.gpsimd.affine_select(out=ident[:], in_=ident[:], compare_op=ALU.not_equal, fill=1.0,
                                    base=0, pattern=[[-1, P]], channel_multiplier=1)
            nc.gpsimd.affine_select(out=mask_even[:, P:], in_=mask_even[:, P:], compare_op=ALU.is_ge,
                                    fill=MASKED, base=0, pattern=[[-1, P]],
                                    channel_multiplier=1).then_inc(const_pool, 1)
            nc.gpsimd.iota(rel_i, pattern=[[-1, 2 * P]], base=P + SEQ, channel_multiplier=1)
            nc.gpsimd.memset(in_window, 1.0).then_inc(iota_ready, 1)
            pool.wait_ge(iota_ready, 1)
            nc.gpsimd.affine_select(out=in_window, in_=in_window, compare_op=ALU.is_ge, fill=0.0, base=0,
                                    pattern=[[1, 2 * P]], channel_multiplier=-1).then_inc(iota_ready, 1)
            pool.wait_ge(ws_loaded, 16)
            nc.gpsimd.affine_select(out=ws, in_=ws, compare_op=ALU.is_ge, fill=0.0, base=0,
                                    pattern=[[0, GROUPS], [-1, P]], channel_multiplier=1).then_inc(ws_masked, 1)
            norms = 0

            def root_of_squares(n):
                pool.wait_ge(squares, n + 1)
                nc.gpsimd.tensor_scalar(sumsq[:, n:n + 1], sumsq[:, n:n + 1], 1.0 / D, EPS, ALU.mult,
                                        ALU.add).then_inc(mean_sq, 1)
                pool.wait_ge(mean_sq, n + 1)
                nc.gpsimd.tensor_tensor(rstd[:, n:n + 1], sumsq[:, n:n + 1], power[:],
                                        ALU.pow).then_inc(rstd_ready, 1)

            root_of_squares(0)
            root_of_squares(1)
            pool.wait_ge(mask_built, 1)
            nc.gpsimd.affine_select(out=mask_odd[:], in_=mask_odd[:], compare_op=ALU.is_ge, fill=MASKED,
                                    base=P, pattern=[[-1, 2 * P]], channel_multiplier=1).then_inc(mask_built, 1)
            for t in range(TILES):
                pool.wait_ge(stats2, t + 1)
                nc.gpsimd.tensor_scalar(meanvar[:, t, 1:2], meanvar[:, t, 1:2], 1.0, 4 * EPS, ALU.mult,
                                        ALU.add).then_inc(ln_plus, 1)
                pool.wait_ge(ln_plus, 2 * t + 1)
                nc.gpsimd.tensor_tensor(rstd[:, 6 + t:7 + t], meanvar[:, t, 1:2], power[:],
                                        ALU.pow).then_inc(ln_plus, 1)
            pool.wait_ge(scores_done, EVEN_HEADS)
            pool.dma_start(gain, norm_g[1:2, :].partition_broadcast(P)).then_inc(gain_loaded[1], 16)
            root_of_squares(2)
            root_of_squares(3)
            pool.wait_ge(scores_done, N_HEADS)
            pool.dma_start(gain, final_norm_g[None, :].partition_broadcast(P)).then_inc(gain_loaded[2], 16)
            root_of_squares(4)
            root_of_squares(5)

        @block.scalar
        def _(act):
            act.dma_start(gain, norm_g[0:1, :].partition_broadcast(P)).then_inc(gain_loaded[0], 16)
            act.dma_start(ws, gmlp_w_s[0].rearrange("g t s -> t g s")).then_inc(ws_loaded, 16)
            act.dma_start(ln_g, gmlp_ln_g.partition_broadcast(P)).then_inc(ln_loaded, 16)
            act.dma_start(ln_b, gmlp_ln_b.partition_broadcast(P)).then_inc(ln_loaded, 16)
            act.dma_start(bias_s[:], gmlp_b_s[0].rearrange("g t -> t g")).then_inc(bias_loaded, 16)

            def square_sum(n):
                t = n % TILES
                nc.scalar.activation(hn[:, t, :], h[:, t, :], ACT.Square,
                                     accum_out=sumsq[:, n:n + 1]).then_inc(squares, 1)

            def hidden_high(n):
                t = n % TILES
                act.wait_ge(hidden_turned, n + 1)
                for i, bank in enumerate((score_banks, (turn_bank, value_bank))[t]):
                    nc.scalar.copy(hnT_hi[:, 4 * i:4 * i + 4, t * P:(t + 1) * P],
                                   bank[:].rearrange("p (a b) -> p a b", b=P)).then_inc(hidden_hi, 1)

            for t in range(TILES):
                act.wait_ge(x_loaded[t], 16)
                square_sum(t)
            for t in range(TILES):
                hidden_high(t)
            act.wait_ge(ws_turned, 1)
            nc.scalar.copy(wsT, banks[3][:].rearrange("p (a b) -> p a b", b=P)).then_inc(wsT_ready, 1)

            for step in order:
                what, n = step[0], step[1]
                if what == "split":
                    half, quarter = n // 2, n % 2
                    act.wait_ge(w_loaded[half % RAW_SLOTS], 16 * (half // RAW_SLOTS + 1))
                    if half >= SPLIT_SLOTS:
                        act.wait_ge(products_done, LAST_ITEM_OF_HALF[half - SPLIT_SLOTS] + 1)
                    part = slice(2 * quarter, 2 * quarter + 2)
                    nc.scalar.copy(w_hi[:, half % SPLIT_SLOTS, part, :],
                                   w_raw[:, half % RAW_SLOTS, part, :]).then_inc(hi_ready, 1)
                elif what == "evacuate":
                    kind, place = GROUPS_OF_BANKS[n]
                    act.wait_ge(products_done, LAST_ITEM_OF_GROUP[n] + 1)
                    if kind in ("query", "key"):
                        to = qT if kind == "query" else kT
                        if kind == "key" and n == 1:
                            act.wait_ge(scaled, TILES)
                        for i, bank in enumerate(pair(n)):
                            c = 4 * place + 2 * i
                            last = nc.scalar.copy(to[:, c:c + 2, :], bank[:].rearrange("p (a b) -> p a b", b=SEQ))
                        last.then_inc(act_emptied, 1)
                    elif kind == "value":
                        for t, bank in enumerate(pair(n)):
                            last = nc.scalar.mul(v[:, t, 0:BLOCK], bank[:], 0.5)
                        last.then_inc(act_emptied, 1)
                    elif kind == "value_tile":
                        for c, bank in enumerate(pair(n)):
                            last = nc.scalar.mul(v[:, place, c * BLOCK:(c + 1) * BLOCK], bank[:], 0.5)
                        last.then_inc(act_emptied, 1)
                    elif kind == "gate":
                        if dve_emptied_before(n):
                            act.wait_ge(dve_emptied, dve_emptied_before(n))
                        for t, bank in enumerate(pair(n)):
                            nc.scalar.activation(tanh[:, t, :], bank[:], ACT.Tanh, scale=0.5).then_inc(tanh_ready, 1)
                elif what == "gelu_inner":
                    act.wait_ge(products_done, LAST_ITEM_OF_GROUP[n] + 1)
                    act.wait_ge(dve_emptied, dve_emptied_before(n))
                    for t, bank in enumerate(pair(n)):
                        nc.scalar.activation(y[:, t, 0:BLOCK], bank[:], ACT.Square).then_inc(squared, 1)
                elif what == "gelu_outer":
                    first = TILES * sum(k == "gelu" for k, _ in GROUPS_OF_BANKS[:n])
                    for t in range(TILES):
                        act.wait_ge(inner_ready, first + t + 1)
                        nc.scalar.activation(tanh[:, t, :], y[:, t, 0:BLOCK], ACT.Tanh).then_inc(tanh_ready, 1)
                elif what == "scores":
                    act.wait_ge(masked, n + 1)
                    for t, (a, b) in enumerate(((0, P), (P, 3 * P))):
                        last = nc.scalar.activation(probs[:, n % 2, a:b], probs[:, n % 2, a:b], ACT.Exp,
                                                    scale=-1.0, bias=least[:, n, t:t + 1],
                                                    accum_out=den[:, n, t:t + 1])
                    last.then_inc(probs_ready, 1)
                elif what == "transpose":
                    act.wait_ge(probs_turned, n + 1)
                    if n >= 2:
                        act.wait_ge(values_done, n - 1)
                    nc.scalar.copy(probsT[:, n % 2, :], turn_bank[:, 0:3 * P]).then_inc(probsT_ready, 1)
                elif what == "y_chunk":
                    act.wait_ge(y_turned, n + 1)
                    chunk = y_place(n)[0]
                    nc.scalar.copy(yT_hi[:, chunk, :], y_place(n)[1]).then_inc(y_hi, 1)
                elif what == "residual":
                    act.wait_ge(added, n + 1)
                    square_sum(n + 2)
                elif what == "hidden":
                    hidden_high(n)

        @block.vector
        def _(dve):
            def chain(instruction, semaphore, value):
                instruction.then_inc(semaphore, 1)
                dve.wait_ge(semaphore, value)

            dve.wait_ge(iota_ready, 2)
            nc.vector.tensor_scalar(rel4, rel_i, 3, None, ALU.bitwise_and)
            chain(nc.vector.tensor_scalar(rel16, rel_i, 15, None, ALU.bitwise_and), mask_count, 1)
            nc.vector.tensor_scalar(part_a, rel4, 0.0, None, ALU.is_equal)
            chain(nc.vector.tensor_scalar(part_b, rel16, 0.0, None, ALU.is_equal), mask_count, 2)
            chain(nc.vector.tensor_tensor(n_held, part_a, part_b, ALU.add), mask_count, 3)
            chain(nc.vector.tensor_tensor(n_held, n_held, in_window, ALU.add), mask_count, 4)
            nc.vector.tensor_scalar(part_a, n_held, 2.0, math.log(2.0) / SCALE, ALU.is_equal, ALU.mult)
            nc.vector.tensor_scalar(part_b, n_held, 3.0, math.log(3.0) / SCALE, ALU.is_equal, ALU.mult)
            chain(nc.vector.tensor_scalar(mask_odd[:], n_held, 0.5, MASKED, ALU.is_lt, ALU.mult), mask_count, 5)
            chain(nc.vector.tensor_tensor(mask_odd[:], mask_odd[:], part_a, ALU.add), mask_count, 6)
            nc.vector.tensor_tensor(mask_odd[:], mask_odd[:], part_b, ALU.add).then_inc(mask_built, 1)

            def scale_tile(n):
                t = n % TILES
                dve.wait_ge(rstd_ready, n + 1)
                dve.wait_ge(gain_loaded[n // TILES], 16)
                nc.vector.scalar_tensor_tensor(out=hn[:, t, :], in0=h[:, t, :], scalar=rstd[:, n:n + 1],
                                               in1=gain, op0=ALU.mult, op1=ALU.mult).then_inc(scaled, 1)

            def hidden_low(n):
                t = n % TILES
                for i, bank in enumerate((score_banks, (turn_bank, value_bank))[t]):
                    dve.wait_ge(hidden_hi, 2 * n + i + 1)
                    place = (slice(None), slice(4 * i, 4 * i + 4), slice(t * P, (t + 1) * P))
                    last = nc.vector.tensor_tensor(hnT_lo[place], bank[:].rearrange("p (a b) -> p a b", b=P),
                                                   hnT_hi[place].bitcast(fp32), ALU.subtract)
                last.then_inc(hidden_ready, 1)

            scale_tile(0)
            scale_tile(1)
            hidden_low(0)
            hidden_low(1)
            gatings = 0
            for step in order:
                what, n = step[0], step[1]
                if what == "split":
                    half, quarter = n // 2, n % 2
                    dve.wait_ge(hi_ready, n + 1)
                    part = slice(2 * quarter, 2 * quarter + 2)
                    nc.vector.tensor_tensor(w_lo[:, half % SPLIT_SLOTS, part, :], w_raw[:, half % RAW_SLOTS, part, :],
                                            w_hi[:, half % SPLIT_SLOTS, part, :].bitcast(fp32),
                                            ALU.subtract).then_inc(lo_ready, 1)
                elif what == "evacuate" and GROUPS_OF_BANKS[n][0] == "gate":
                    for t, bank in enumerate(pair(n)):
                        dve.wait_ge(tanh_ready, tanh_writes_before(n) + t + 1)
                        last = nc.vector.scalar_tensor_tensor(
                            out=gate[:, GROUPS_OF_BANKS[n][1], t, :], in0=tanh[:, t, :], scalar=1.0, in1=bank[:],
                            op0=ALU.add, op1=ALU.mult)
                    last.then_inc(dve_emptied, 1)
                elif what == "gelu_inner":
                    first = TILES * sum(k == "gelu" for k, _ in GROUPS_OF_BANKS[:n])
                    for t, bank in enumerate(pair(n)):
                        dve.wait_ge(squared, first + t + 1)
                        chain(nc.vector.tensor_scalar(y[:, t, 0:BLOCK], y[:, t, 0:BLOCK], GELU_C * GELU_A, GELU_C,
                                                      ALU.mult, ALU.add), poly, first + t + 1)
                        nc.vector.tensor_tensor(y[:, t, 0:BLOCK], y[:, t, 0:BLOCK], bank[:],
                                                ALU.mult).then_inc(inner_ready, 1)
                elif what == "gelu_outer":
                    place = GROUPS_OF_BANKS[n][1] * BLOCK
                    for t, bank in enumerate(pair(n)):
                        dve.wait_ge(tanh_ready, tanh_writes_before(n) + t + 1)
                        last = nc.vector.scalar_tensor_tensor(
                            out=hn[:, t, place:place + BLOCK], in0=tanh[:, t, :], scalar=1.0, in1=bank[:],
                            op0=ALU.add, op1=ALU.mult)
                    last.then_inc(dve_emptied, 1)
                elif what == "layer_norm":
                    vt = hn[:, n, BLOCK:D]
                    dve.wait_ge(dve_emptied, dve_emptied_before(4) + 1)
                    chain(nc.vector.bn_stats(moments[:, n, :], vt), stats, n + 1)
                    nc.vector.bn_aggr(meanvar[:, n, :], moments[:, n, :]).then_inc(stats2, 1)
                    dve.wait_ge(ln_plus, 2 * n + 2)
                    dve.wait_ge(ln_loaded, 32)
                    chain(nc.vector.tensor_scalar(vt, vt, meanvar[:, n, 0:1], rstd[:, 6 + n:7 + n], ALU.subtract,
                                                  ALU.mult), centred, n + 1)
                    chain(nc.vector.tensor_tensor(vt, vt, ln_g, ALU.mult), gained, n + 1)
                    nc.vector.tensor_tensor(vt, vt, ln_b, ALU.add).then_inc(v_normed, 1)
                elif what == "mix_u":
                    dve.wait_ge(mix_done, n + 1)
                    dve.wait_ge(bias_loaded, 16)
                    dve.wait_ge(dve_emptied, dve_emptied_before(5) + 1)
                    for g in range(GROUPS):
                        cols = slice(g * P, (g + 1) * P)
                        last = nc.vector.scalar_tensor_tensor(
                            out=y[:, n, cols], in0=score_banks[n][:, cols], scalar=bias_s[:, g:g + 1],
                            in1=hn[:, n, cols], op0=ALU.add, op1=ALU.mult)
                    last.then_inc(mixed, 1)
                elif what == "gating":
                    for t in range(TILES):
                        if n == 1:
                            dve.wait_ge(mixed, TILES)
                            dve.wait_ge(dve_emptied, dve_emptied_before(6) + 1)
                            last = nc.vector.scalar_tensor_tensor(
                                out=y[:, t, 0:BLOCK], in0=y[:, t, 0:BLOCK], scalar=0.25, in1=gate[:, 0, t, :],
                                op0=ALU.mult, op1=ALU.mult)
                        else:
                            c = {0: 1, 2: 0, 3: 1}[n]
                            dve.wait_ge(attended, {0: EVEN_HEADS, 2: EVEN_HEADS + 8, 3: N_HEADS}[n])
                            dve.wait_ge(dve_emptied, dve_emptied_before({0: 3, 2: 15, 3: 16}[n]) + 1)
                            cols = slice((c if n else 1) * BLOCK, (c + 1 if n else 2) * BLOCK)
                            last = nc.vector.tensor_tensor(y[:, t, cols], y[:, t, cols], gate[:, c, t, :], ALU.mult)
                    last.then_inc(gated, 1)
                elif what == "scores":
                    mask = mask_even if n < EVEN_HEADS else mask_odd
                    dve.wait_ge(scores_done, n + 1)
                    if n in (0, EVEN_HEADS):
                        dve.wait_ge(const_pool, 2)
                        dve.wait_ge(mask_built, 2)
                    if n >= 2:
                        dve.wait_ge(probs_turned, n - 1)
                    for t, (a, b) in enumerate(((0, P), (P, 3 * P))):
                        last = nc.vector.tensor_tensor_reduce(
                            out=probs[:, n % 2, a:b], in0=score_banks[n % 2][:, a:b], in1=mask[:, 2 * P - (b - a):],
                            scale=-SCALE, scalar=3e38, op0=ALU.add, op1=ALU.min, accum_out=least[:, n, t:t + 1])
                    last.then_inc(masked, 1)
                elif what == "values":
                    dve.wait_ge(values_done, n + 1)
                    chain(nc.vector.reciprocal(rden[:, n, :], den[:, n, :]), inverted, n + 1)
                    column = head_place(n)[2] + (BLOCK if n < EVEN_HEADS else 0)
                    for t in range(TILES):
                        at = (n % 2) * P + t * HEAD
                        last = nc.vector.tensor_scalar(y[:, t, column:column + HEAD], value_bank[:, at:at + HEAD],
                                                       rden[:, n, t:t + 1], None, ALU.mult)
                    last.then_inc(attended, 1)
                elif what == "y_chunk":
                    chunk, place, _ = y_place(n)
                    dve.wait_ge(y_hi, n + 1)
                    nc.vector.tensor_tensor(yT_lo[:, chunk, :], place, yT_hi[:, chunk, :].bitcast(fp32),
                                            ALU.subtract).then_inc(y_lo, 1)
                elif what == "residual":
                    layer, t = n // TILES, n % TILES
                    group = (7, 17)[layer] + t
                    dve.wait_ge(products_done, LAST_ITEM_OF_GROUP[group] + 1)
                    for c, bank in enumerate(pair(group)):
                        cols = slice(c * BLOCK, (c + 1) * BLOCK)
                        last = nc.vector.tensor_tensor(h[:, t, cols], h[:, t, cols], bank[:], ALU.add)
                    last.then_inc(added, 1)
                elif what == "scale":
                    scale_tile(2 + n)
                elif what == "hidden":
                    hidden_low(n)
                elif what == "final":
                    scale_tile(4 + n)

        @block.tensor
        def _(pe):
            def turn(to, of):
                return nc.tensor.matmul(to, of, ident[:], is_transpose=True, start=True, stop=True)

            def hidden_turn(n):
                t = n % TILES
                pe.wait_ge(scaled, n + 1)
                for i, bank in enumerate((score_banks, (turn_bank, value_bank))[t]):
                    for c in range(4):
                        last = turn(bank[:, c * P:(c + 1) * P], hn[:, t, (4 * i + c) * P:(4 * i + c + 1) * P])
                last.then_inc(hidden_turned, 1)

            pe.wait_ge(const_pool, 2)
            hidden_turn(0)
            hidden_turn(1)
            pe.wait_ge(ws_masked, 1)
            for g in range(GROUPS):
                last = turn(banks[3][:, g * P:(g + 1) * P], ws[:, g, :])
            last.then_inc(ws_turned, 1)
            pe.wait_ge(wsT_ready, 1)
            pe.wait_ge(hidden_ready, TILES)

            started = set()
            heads_valued = chunks_turned = 0
            for step in order:
                what, n = step[0], step[1]
                if what == "product":
                    half_item = step[2]
                    group, half, quarter, side = ITEMS[n]
                    kind, place = GROUPS_OF_BANKS[group]
                    matrix, chunk0, _ = HALVES[half]
                    if half_item == 0:
                        pe.wait_ge(lo_ready, 2 * half + quarter + 1)
                        if group >= 2 and group not in started:
                            wait_emptied(pe, group - 2)
                        started.add(group)
                        if kind == "residual":
                            layer = 0 if matrix == "even_out" else 1
                            first = chunk0 + 2 * quarter
                            order_of = {c: i for i, c in enumerate((4, 5, 6, 7, 0, 1, 2, 3) if layer == 0
                                                                   else range(CHUNKS))}
                            pe.wait_ge(y_lo, CHUNKS * layer + max(order_of[first], order_of[first + 1]) + 1)
                        if kind == "value_tile":
                            pe.wait_ge(hidden_ready, TILES + place + 1)
                    hi, lo = (yT_hi, yT_lo) if kind == "residual" else (hnT_hi, hnT_lo)
                    r = 2 * quarter + half_item
                    chunk = chunk0 + r
                    slot = half % SPLIT_SLOTS
                    begins = chunk == (HALF_CHUNKS if matrix == "even_out" else 0)
                    ends = chunk == (HALF_CHUNKS - 1 if matrix == "even_out" else CHUNKS - 1)
                    if kind in ("query", "key"):
                        for c in range(4):
                            to = pair(group)[c // 2][:, (c % 2) * SEQ:(c % 2 + 1) * SEQ]
                            cols = slice(c * P, (c + 1) * P)
                            wh, wl = w_hi[:, slot, r, cols], w_lo[:, slot, r, cols]
                            nc.tensor.matmul(to, wh, hi[:, chunk, :], start=begins and c % 2 == 0, stop=False,
                                             skip_group_check=True)
                            nc.tensor.matmul(to, wh, lo[:, chunk, :], start=False, stop=False,
                                             skip_group_check=True)
                            last = nc.tensor.matmul(to, wl, hi[:, chunk, :], start=False, stop=ends,
                                                    skip_group_check=True)
                    else:
                        if side is None:
                            targets = [(t, pair(group)[t]) for t in range(TILES)]
                        else:
                            targets = [(place, pair(group)[side])]
                        for t, to in targets:
                            rows = slice(t * P, (t + 1) * P)
                            xh, xl = hi[:, chunk, rows], lo[:, chunk, rows]
                            nc.tensor.matmul(to[:], xh, w_hi[:, slot, r, :], start=begins, stop=False)
                            nc.tensor.matmul(to[:], xl, w_hi[:, slot, r, :], start=False, stop=False)
                            last = nc.tensor.matmul(to[:], xh, w_lo[:, slot, r, :], start=False, stop=ends)
                    if half_item == 1:
                        last.then_inc(products_done, 1)
                elif what == "scores":
                    chunk, row, _ = head_place(n)
                    if n == 0:
                        pe.wait_ge(act_emptied, 2)
                    elif n in (EVEN_HEADS, EVEN_HEADS + 8):
                        pe.wait_ge(act_emptied, count_of_kind(ACT_KINDS, 12 if n == EVEN_HEADS else 14))
                    if n >= 2:
                        pe.wait_ge(masked, n - 1)
                    q, k = qT[row:row + HEAD, chunk, :], kT[row:row + HEAD, chunk, :]
                    bank = score_banks[n % 2]
                    nc.tensor.matmul(bank[:, 0:P], q[:, 0:P], k[:, 0:P], start=True, stop=True)
                    nc.tensor.matmul(bank[:, P:3 * P], q[:, P:SEQ], k, start=True, stop=True).then_inc(scores_done, 1)
                elif what == "transpose":
                    pe.wait_ge(probs_ready, n + 1)
                    if n >= 1:
                        pe.wait_ge(probsT_ready, n)
                    for i in range(3):
                        last = turn(turn_bank[:, i * P:(i + 1) * P], probs[:, n % 2, i * P:(i + 1) * P])
                    last.then_inc(probs_turned, 1)
                elif what == "values":
                    pe.wait_ge(probsT_ready, n + 1)
                    if n >= 1:
                        pe.wait_ge(attended, n)
                    if chunks_turned:
                        pe.wait_ge(y_lo, chunks_turned)
                    heads_valued = n + 1
                    column = head_place(n)[2]
                    at = (n % 2) * P
                    pT = probsT[:, n % 2, :]
                    v0, v1 = v[:, 0, column:column + HEAD], v[:, 1, column:column + HEAD]
                    nc.tensor.matmul(value_bank[:, at:at + HEAD], pT[:, 0:P], v0, start=True, stop=True)
                    to = value_bank[:, at + HEAD:at + 2 * HEAD]
                    nc.tensor.matmul(to, pT[:, P:2 * P], v0, start=True, stop=False)
                    nc.tensor.matmul(to, pT[:, 2 * P:3 * P], v1, start=False, stop=True).then_inc(values_done, 1)
                elif what == "mix":
                    pe.wait_ge(v_normed, n + 1)
                    pe.wait_ge(masked, EVEN_HEADS)
                    for g in range(GROUPS):
                        cols = slice(BLOCK + g * P, BLOCK + (g + 1) * P)
                        last = nc.tensor.matmul(score_banks[n][:, g * P:(g + 1) * P], wsT[:, g, :], hn[:, n, cols],
                                                start=True, stop=True)
                    last.then_inc(mix_done, 1)
                elif what == "y_chunk":
                    chunk, place, alone = y_place(n)
                    pe.wait_ge(gated, n // 4 + 1)
                    before = n - 1 if alone else n - 2
                    if n % 4 == 0:
                        before = n - 1
                    if before >= 0:
                        pe.wait_ge(y_lo, before + 1)
                    pe.wait_ge(attended, heads_valued)
                    chunks_turned = n + 1
                    if n % 4 == 1:
                        pe.wait_ge(probsT_ready, {1: EVEN_HEADS, 5: EVEN_HEADS, 9: EVEN_HEADS, 13: N_HEADS}[n])
                    for t in range(TILES):
                        last = turn(place[:, t * P:(t + 1) * P], y[:, t, chunk * P:(chunk + 1) * P])
                    last.then_inc(y_turned, 1)
                elif what == "hidden":
                    if n == 2:
                        pe.wait_ge(mixed, TILES)
                    hidden_turn(n)


_NAMES = ("x", "norm_g", "final_norm_g", "ab_w_in", "ab_w_out", "gmlp_ln_g", "gmlp_ln_b", "gmlp_w_s", "gmlp_b_s",
          "c_w_in", "c_w_out")


def kernel(**inputs):
    import numpy as np
    import concourse.bacc as bacc
    from concourse.bass_utils import run_bass_kernel_spmd

    nc = bacc.Bacc("TRN2", target_bir_lowering=False, num_devices=1)
    arrays, args = {}, []
    for name in _NAMES:
        a = np.ascontiguousarray(inputs[name])
        arrays[f"in_{name}"] = a
        args.append(nc.dram_tensor(f"in_{name}", a.shape, mybir.dt.from_np(a.dtype), kind="ExternalInput").ap())
    out = nc.dram_tensor("out_0", (1, SEQ, D), mybir.dt.float32, kind="ExternalOutput").ap()
    build(nc, *args, out)
    result = run_bass_kernel_spmd(nc, [arrays], core_ids=[0])
    return result.results[0]["out_0"]
```

```python
import math
from contextlib import ExitStack

import concourse.bass as bass
from concourse import mybir
from concourse.alu_op_type import AluOpType as ALU

P = 128
SEQ = 256
TILES = SEQ // P
D = 1024
CHUNKS = D // P
BLOCK = 512
HALF_CHUNKS = CHUNKS // 2
HEAD = 64
EVEN_HEADS = 8
ODD_HEADS = 16
GROUPS = 4
EPS = 1e-6
SCALE = HEAD ** -0.5
MASKED = -1e30
GELU_C = math.sqrt(2.0 / math.pi)
GELU_A = 0.044715
RAW_SLOTS = 3
SPLIT_SLOTS = 5


SOON, AHEAD, MOST_TURNS, LAG = 3, 12, 1.5, 1


def plan():
    halves, groups, items = [], [], []

    def whole(matrix, column, kind, place):
        g = len(groups)
        groups.append((kind, place))
        for part in range(2):
            h = len(halves)
            halves.append((matrix, part * HALF_CHUNKS, column))
            items.extend((g, h, q, None) for q in range(2))

    def output(matrix, parts):
        g = len(groups)
        groups.extend([("residual", 0), ("residual", 1)])
        for part in parts:
            h = len(halves)
            halves.extend((matrix, part * HALF_CHUNKS, c * BLOCK) for c in range(2))
            for tile in range(TILES):
                items.extend((g + tile, h + c, q, c) for c in range(2) for q in range(2))

    u, v, ga, q, k, vv, gb = (i * BLOCK for i in range(7))
    whole("even_in", q, "query", 0)
    whole("even_in", k, "key", 0)
    whole("even_in", vv, "value", 0)
    whole("even_in", v, "gelu", 1)
    whole("even_in", gb, "gate", 1)
    whole("even_in", u, "gelu", 0)
    whole("even_in", ga, "gate", 0)
    output("even_out", (1, 0))
    g, h = len(groups), len(halves)
    groups.extend([("value_tile", 0), ("value_tile", 1)])
    halves.extend(("odd_in", part * HALF_CHUNKS, 2 * D + c * BLOCK) for c in range(2) for part in range(2))
    for tile in range(TILES):
        items.extend((g + tile, h + i, q, i // 2) for i in range(4) for q in range(2))
    for c in range(2):
        whole("odd_in", c * BLOCK, "query", c)
        whole("odd_in", D + c * BLOCK, "key", c)
    for c in range(2):
        whole("odd_in", 3 * D + c * BLOCK, "gate", c)
    output("odd_out", (0, 1))
    return halves, groups, items


HALVES, GROUPS_OF_BANKS, ITEMS = plan()
LAST_ITEM_OF_GROUP = {item[0]: n for n, item in enumerate(ITEMS)}
LAST_ITEM_OF_HALF = {item[1]: n for n, item in enumerate(ITEMS)}
ACT_KINDS = ("query", "key", "value", "value_tile")


def steps():
    out, split = [("hidden", 0), ("round", 0), ("hidden", 1), ("rest", 0)], 1
    first_item = {}
    for n, item in enumerate(ITEMS):
        first_item.setdefault(item[0], n)
    extra = {}

    def at(position, *what):
        extra.setdefault(position, []).extend(what)

    def heads(first_position, numbers, pace):
        for n, head in enumerate(numbers):
            p = first_position + pace(n)
            at(p, ("scores", head))
            at(p + 3, ("transpose", head))
            if head % 2:
                at(p + 5, ("values", head // 2))

    even_attention = 2 * first_item[3]
    at(even_attention - 8, ("ws", 0))
    heads(even_attention, range(EVEN_HEADS), lambda n: 2 * n)
    at(2 * first_item[1] + 2, ("windows", 0))
    behind_v = 2 * first_item[4]
    at(behind_v, ("gelu_inner", 3))
    at(behind_v + 1, ("gelu_outer", 3))
    at(behind_v + 3, ("layer_norm", 0))
    at(behind_v + 5, ("layer_norm", 1))
    behind_gb = 2 * first_item[5]
    at(behind_gb + 1, ("mix", 0))
    at(behind_gb + 2, ("mix", 1))
    at(behind_gb + 4, ("gating", 0))
    for i in range(4):
        at(behind_gb + 5 + i, ("y_chunk", i))
    behind_u = 2 * first_item[6]
    at(behind_u, ("gelu_inner", 5))
    at(behind_u + 1, ("gelu_outer", 5))
    at(behind_u + 3, ("mix_u", 0))
    at(behind_u + 5, ("mix_u", 1))
    out_even = 2 * first_item[7]
    at(out_even + 1, ("gating", 1))
    for i in range(4):
        at(out_even + 7 + 2 * i, ("y_chunk", 4 + i))
    v_odd = 2 * first_item[9]
    at(v_odd - 12, ("residual", 0, 0))
    at(v_odd - 8, ("residual", 0, 1), ("scale", 0))
    at(v_odd - 4, ("residual", 1, 0))
    at(v_odd - 1, ("hidden", 2))
    at(v_odd, ("residual", 1, 1), ("scale", 1))
    at(v_odd + 12, ("hidden", 3))
    odd_attention = 2 * first_item[13] + 1
    heads(odd_attention, range(EVEN_HEADS, EVEN_HEADS + 8), lambda n: 2 * n)
    heads(2 * first_item[15] + 1, range(EVEN_HEADS + 8, EVEN_HEADS + 16), lambda n: n + n // 2)
    g0 = 2 * first_item[16]
    at(g0 + 1, ("gating", 2))
    for i in range(4):
        at(g0 + 2 + 2 * i, ("y_chunk", 8 + i))
    out_odd = 2 * first_item[17]
    at(out_odd + 3, ("gating", 3))
    for i in range(4):
        at(out_odd + 7 + 2 * i, ("y_chunk", 12 + i))

    end = 2 * len(ITEMS)
    at(end - 12, ("residual", 2, 0))
    at(end - 8, ("residual", 2, 1), ("scale", 2))
    at(end - 4, ("residual", 3, 0))

    first_use = {}
    for n, item in enumerate(ITEMS):
        first_use.setdefault(2 * item[1] + item[2], n)
    freed, turns, rounded = {}, 0.0, []
    for n, item in enumerate(ITEMS):
        turns = min(turns + (1.0 if item[3] is None else 0.5), MOST_TURNS)
        for half in range(2):
            while half == 0 and split < 2 * len(HALVES):
                soon = first_use[split] <= n + SOON
                before = split // 2 - SPLIT_SLOTS
                if before >= 0 and freed.get(before, n) > n - (1 if soon else 2):
                    break
                if not soon and (turns < 1.0 or first_use[split] > n + AHEAD):
                    break
                out.append(("round", split))
                rounded.append(split)
                split += 1
                turns = max(turns - 1.0, -1.0)
            while rounded and (len(rounded) > LAG or first_use[rounded[0]] <= n + 1):
                out.append(("rest", rounded.pop(0)))
            out.extend(extra.pop(2 * n + half, ()))
            out.append(("product", n, half))
        for h, last in LAST_ITEM_OF_HALF.items():
            if last == n:
                freed[h] = n
        g = item[0]
        if LAST_ITEM_OF_GROUP[g] == n and GROUPS_OF_BANKS[g][0] not in ("gelu", "residual"):
            out.append(("evacuate", g))
    assert not extra, extra
    out.extend([("residual", 3, 1), ("scale", 3)])
    return out


def count_of_kind(kinds, group):
    return sum(k in kinds for k, _ in GROUPS_OF_BANKS[: group + 1])


def build(nc, x, norm_g, final_norm_g, ab_w_in, ab_w_out, gmlp_ln_g, gmlp_ln_b, gmlp_w_s, gmlp_b_s,
          c_w_in, c_w_out, out):
    fp32 = mybir.dt.float32
    fp32r = mybir.dt.float32r
    int32 = mybir.dt.int32
    ACT = mybir.ActivationFunctionType
    matrices = {"even_in": ab_w_in[0], "even_out": ab_w_out[0], "odd_in": c_w_in[0], "odd_out": c_w_out[0]}
    order = steps()
    x_tiles = x[0].rearrange("(t p) c -> t p c", p=P)
    out_tiles = out[0].rearrange("(t p) c -> t p c", p=P)
    N_HEADS = EVEN_HEADS + ODD_HEADS

    ctx = ExitStack()
    with ctx:
        def sb(name, shape, dtype=fp32):
            return ctx.enter_context(nc.sbuf_tensor(name, shape, dtype))

        def sem(name):
            return ctx.enter_context(nc.semaphore(name))

        ctx.enter_context(nc.allow_non_contiguous_dma(reason="a bias of 512 numbers, once"))
        w_raw = sb("w_raw", [P, RAW_SLOTS, HALF_CHUNKS, BLOCK])
        w_hi = sb("w_hi", [P, SPLIT_SLOTS, HALF_CHUNKS, BLOCK], fp32r)
        w_lo = sb("w_lo", [P, SPLIT_SLOTS, HALF_CHUNKS, BLOCK], fp32r)
        h = sb("h", [P, TILES, D])
        hn = sb("hn", [P, TILES, D])
        hnT_hi = sb("hnT_hi", [P, CHUNKS, SEQ], fp32r)
        hnT_lo = sb("hnT_lo", [P, CHUNKS, SEQ], fp32r)
        yT_hi = sb("yT_hi", [P, CHUNKS, SEQ], fp32r)
        yT_lo = sb("yT_lo", [P, CHUNKS, SEQ], fp32r)
        qT = sb("qT", [P, CHUNKS, SEQ])
        kT = sb("kT", [P, CHUNKS, SEQ])
        v = sb("v", [P, TILES, D])
        gate = sb("gate", [P, 2, TILES, BLOCK])
        y = sb("y", [P, TILES, D])
        tanh = sb("tanh", [P, TILES, BLOCK])
        probs = sb("probs", [P, 2, 3 * P])
        probsT = sb("probsT", [P, 2, 3 * P])
        least = sb("least", [P, N_HEADS, 2])
        den = sb("den", [P, N_HEADS, 2])
        rden = sb("rden", [P, N_HEADS, 2])
        mask_even = sb("mask_even", [P, 2 * P])
        mask_odd = sb("mask_odd", [P, 2 * P])
        ident = sb("ident", [P, P])
        bias_s = sb("bias_s", [P, GROUPS])
        sumsq = sb("sumsq", [P, 6, 2])
        rstd = sb("rstd", [P, 8])
        power = sb("power", [P, 1])
        moments = sb("moments", [P, TILES, nc.vector.BN_STATS_DIM])
        meanvar = sb("meanvar", [P, TILES, nc.vector.BN_AGGR_DIM])
        gain = kT[:, 0:4, :].rearrange("p a b -> p (a b)")
        ws = qT[:, 4:6, :].rearrange("p a (b s) -> p (a b) s", s=P)
        wsT = kT[:, 4:6, :].rearrange("p a (b t) -> p (a b) t", t=P)
        ln_g, ln_b = v[:, 0, BLOCK:D], v[:, 1, BLOCK:D]
        rel = probs[:, :, 0:P].bitcast(int32)
        rel4 = gate[:, 0, 0, 0:2 * P].bitcast(int32)
        rel16 = gate[:, 0, 0, 2 * P:4 * P].bitcast(int32)
        rel_i = gate[:, 1, 0, 0:2 * P].bitcast(int32)
        n_held = gate[:, 1, 1, 0:2 * P]
        part_a = gate[:, 0, 1, 0:2 * P]
        part_b = gate[:, 0, 1, 2 * P:4 * P]
        in_window = gate[:, 1, 1, 2 * P:4 * P]

        banks = [ctx.enter_context(nc.psum_tensor(f"products{i}", [P, BLOCK], fp32)) for i in range(4)]
        score_banks = [ctx.enter_context(nc.psum_tensor(f"scores{i}", [P, BLOCK], fp32)) for i in range(2)]
        turn_bank = ctx.enter_context(nc.psum_tensor("turned", [P, BLOCK], fp32))
        value_bank = ctx.enter_context(nc.psum_tensor("attended", [P, BLOCK], fp32))
        free_half = value_bank[:, 2 * P:4 * P]

        w_loaded = [sem(f"w_loaded{i}") for i in range(RAW_SLOTS)]
        x_loaded = [sem(f"x_loaded{i}") for i in range(TILES)]
        gain_loaded = [sem(f"gain_loaded{i}") for i in range(3)]
        ws_loaded, ln_loaded, bias_loaded = sem("ws_loaded"), sem("ln_loaded"), sem("bias_loaded")
        stored = sem("stored")
        hi_ready, lo_ready = sem("hi_ready"), sem("lo_ready")
        products_done = sem("products_done")
        act_emptied, dve_emptied = sem("act_emptied"), sem("dve_emptied")
        const_pool, const_dve = sem("const_pool"), sem("const_dve")
        iota_ready, mask_count = sem("iota_ready"), sem("mask_count")
        mask_built = sem("mask_built")
        ws_masked, ws_turned, wsT_ready = sem("ws_masked"), sem("ws_turned"), sem("wsT_ready")
        squares, sum_sq, mean_sq, rstd_ready = sem("squares"), sem("sum_sq"), sem("mean_sq"), sem("rstd_ready")
        with_gain, final_act = sem("with_gain"), sem("final_act")
        w_first, table = sem("w_first"), sem("table")
        added, scaled = sem("added"), sem("scaled")
        hidden_turned, hidden_hi, hidden_ready = sem("hidden_turned"), sem("hidden_hi"), sem("hidden_ready")
        scores_done, masked, probs_ready = sem("scores_done"), sem("masked"), sem("probs_ready")
        probs_turned, probsT_ready = sem("probs_turned"), sem("probsT_ready")
        values_done, inverted, attended = sem("values_done"), sem("inverted"), sem("attended")
        squared, inner_ready = sem("squared"), sem("inner_ready")
        tanh_ready = sem("tanh_ready")
        stats, stats2, centred, v_normed = sem("stats"), sem("stats2"), sem("centred"), sem("v_normed")
        ln_plus = sem("ln_plus")
        mix_done, mixed = sem("mix_done"), sem("mixed")
        gated = sem("gated")
        y_turned, y_hi, y_lo = sem("y_turned"), sem("y_hi"), sem("y_lo")

        def pair(group):
            return banks[2 * (group % 2)], banks[2 * (group % 2) + 1]

        def wait_emptied(engine, group):
            if GROUPS_OF_BANKS[group][0] in ACT_KINDS:
                engine.wait_ge(act_emptied, count_of_kind(ACT_KINDS, group))
            elif GROUPS_OF_BANKS[group][0] == "residual":
                engine.wait_ge(added, 2 * count_of_kind(("residual",), group))
            else:
                engine.wait_ge(dve_emptied, count_of_kind(("gate", "gelu"), group))

        def dve_emptied_before(group):
            return count_of_kind(("gate", "gelu"), group - 1)

        def tanh_writes_before(group):
            return TILES * dve_emptied_before(group)

        def head_place(head):
            n = head if head < EVEN_HEADS else head - EVEN_HEADS
            return n // 2, HEAD * (n % 2), HEAD * n

        def y_place(n):
            chunk = (4, 5, 6, 7, 0, 1, 2, 3)[n] if n < CHUNKS else n - CHUNKS
            alone = n in range(8, 12)
            return chunk, (free_half if n % 2 == 0 or alone else turn_bank[:, 0:2 * P]), alone

        block = ctx.enter_context(nc.Block())

        @block.sync
        def _(sp):
            sp.dma_start(h[:, 0, :], x_tiles[0]).then_inc(x_loaded[0], 16)
            sp.dma_start(h[:, 1, :], x_tiles[1]).then_inc(x_loaded[1], 16)
            sp.dma_start(gain, norm_g[0:1, :].partition_broadcast(P)).then_inc(gain_loaded[0], 16)
            for n, (matrix, chunk, column) in enumerate(HALVES):
                if n >= RAW_SLOTS:
                    sp.wait_ge(lo_ready, 2 * (n - RAW_SLOTS + 1))
                rows = matrices[matrix][chunk * P:(chunk + HALF_CHUNKS) * P, column:column + BLOCK]
                rows = rows.rearrange("(k p) c -> p k c", p=P)
                if n == 0:
                    sp.dma_start(w_raw[:, 0, 0:2], rows[:, 0:2]).then_inc(w_first, 16)
                    sp.dma_start(w_raw[:, 0, 2:4], rows[:, 2:4]).then_inc(w_loaded[0], 16)
                    continue
                sp.dma_start(w_raw[:, n % RAW_SLOTS], rows).then_inc(w_loaded[n % RAW_SLOTS], 16)
                if n == 2:
                    sp.dma_start(ws, gmlp_w_s[0].rearrange("g t s -> t g s")).then_inc(ws_loaded, 16)
                    sp.dma_start(ln_g, gmlp_ln_g.partition_broadcast(P)).then_inc(ln_loaded, 16)
                    sp.dma_start(ln_b, gmlp_ln_b.partition_broadcast(P)).then_inc(ln_loaded, 16)
                    sp.dma_start(bias_s[:], gmlp_b_s[0].rearrange("g t -> t g")).then_inc(bias_loaded, 16)
            for t in range(TILES):
                sp.wait_ge(scaled, 2 * 2 * TILES + t + 1)
                sp.dma_start(out_tiles[t][:, 0:BLOCK], hn[:, t, 0:BLOCK]).then_inc(stored, 16)
                sp.wait_ge(final_act, t + 1)
                sp.dma_start(out_tiles[t][:, BLOCK:D], hn[:, t, BLOCK:D]).then_inc(stored, 16)
            sp.wait_ge(stored, 16 * 2 * TILES)

        @block.gpsimd
        def _(pool):
            nc.gpsimd.memset(power[:], -0.5)
            nc.gpsimd.memset(ident[:], 0.0)
            nc.gpsimd.memset(mask_even[:], 0.0).then_inc(const_pool, 1)
            pool.wait_ge(const_pool, 1)
            nc.gpsimd.affine_select(out=ident[:], in_=ident[:], compare_op=ALU.not_equal, fill=1.0,
                                    base=0, pattern=[[-1, P]], channel_multiplier=1)
            nc.gpsimd.affine_select(out=mask_even[:, P:], in_=mask_even[:, P:], compare_op=ALU.is_ge,
                                    fill=MASKED, base=0, pattern=[[-1, P]],
                                    channel_multiplier=1).then_inc(const_pool, 1)
            nc.gpsimd.iota(rel_i, pattern=[[-1, 2 * P]], base=P + SEQ, channel_multiplier=1)
            nc.gpsimd.memset(in_window, 1.0).then_inc(iota_ready, 1)
            pool.wait_ge(iota_ready, 1)
            nc.gpsimd.affine_select(out=in_window, in_=in_window, compare_op=ALU.is_ge, fill=0.0, base=0,
                                    pattern=[[1, 2 * P]], channel_multiplier=-1).then_inc(iota_ready, 1)

            def root_of_squares(n):
                total = sumsq[:, n, 0:1]
                pool.wait_ge(squares, 2 * n + 2)
                nc.gpsimd.tensor_tensor(total, total, sumsq[:, n, 1:2], ALU.add).then_inc(sum_sq, 1)
                pool.wait_ge(sum_sq, n + 1)
                nc.gpsimd.tensor_scalar(total, total, 1.0 / D, EPS, ALU.mult, ALU.add).then_inc(mean_sq, 1)
                pool.wait_ge(mean_sq, n + 1)
                nc.gpsimd.tensor_tensor(rstd[:, n:n + 1], total, power[:], ALU.pow).then_inc(rstd_ready, 1)

            root_of_squares(0)
            root_of_squares(1)
            pool.wait_ge(ws_loaded, 16)
            nc.gpsimd.affine_select(out=ws, in_=ws, compare_op=ALU.is_ge, fill=0.0, base=0,
                                    pattern=[[0, GROUPS], [-1, P]], channel_multiplier=1).then_inc(ws_masked, 1)
            pool.wait_ge(mask_built, 1)
            nc.gpsimd.affine_select(out=mask_odd[:], in_=mask_odd[:], compare_op=ALU.is_ge, fill=MASKED,
                                    base=P, pattern=[[-1, 2 * P]], channel_multiplier=1).then_inc(mask_built, 1)
            for t in range(TILES):
                pool.wait_ge(stats2, t + 1)
                nc.gpsimd.tensor_scalar(meanvar[:, t, 1:2], meanvar[:, t, 1:2], 1.0, 4 * EPS, ALU.mult,
                                        ALU.add).then_inc(ln_plus, 1)
                pool.wait_ge(ln_plus, 2 * t + 1)
                nc.gpsimd.tensor_tensor(rstd[:, 6 + t:7 + t], meanvar[:, t, 1:2], power[:],
                                        ALU.pow).then_inc(ln_plus, 1)
            pool.wait_ge(scores_done, EVEN_HEADS)
            pool.dma_start(gain, norm_g[1:2, :].partition_broadcast(P)).then_inc(gain_loaded[1], 16)
            root_of_squares(2)
            root_of_squares(3)
            pool.wait_ge(scores_done, N_HEADS)
            pool.dma_start(gain, final_norm_g[None, :].partition_broadcast(P)).then_inc(gain_loaded[2], 16)
            root_of_squares(4)
            root_of_squares(5)

        @block.scalar
        def _(act):
            act.wait_ge(const_pool, 1)
            nc.scalar.activation(rstd[:, 0:1], power[:], ACT.Tanh).then_inc(table, 1)

            def square_sum(n, c):
                t = n % TILES
                nc.scalar.activation(tanh[:, t, :], h[:, t, c * BLOCK:(c + 1) * BLOCK], ACT.Square,
                                     accum_out=sumsq[:, n, c:c + 1]).then_inc(squares, 1)

            def hidden_high(n):
                t = n % TILES
                for i, bank in enumerate((score_banks, (turn_bank, value_bank))[t]):
                    act.wait_ge(hidden_turned, 2 * n + i + 1)
                    nc.scalar.copy(hnT_hi[:, 4 * i:4 * i + 4, t * P:(t + 1) * P],
                                   bank[:].rearrange("p (a b) -> p a b", b=P)).then_inc(hidden_hi, 1)

            for t in range(TILES):
                act.wait_ge(x_loaded[t], 16)
                for c in range(2):
                    if t or c:
                        act.wait_ge(squares, 2 * t + c)
                    square_sum(t, c)
            for step in order:
                what, n = step[0], step[1]
                if what == "round":
                    half, quarter = n // 2, n % 2
                    if n == 0:
                        act.wait_ge(w_first, 16)
                    else:
                        act.wait_ge(w_loaded[half % RAW_SLOTS], 16 * (half // RAW_SLOTS + 1))
                    if half >= SPLIT_SLOTS:
                        act.wait_ge(products_done, LAST_ITEM_OF_HALF[half - SPLIT_SLOTS] + 1)
                    part = slice(2 * quarter, 2 * quarter + 2)
                    nc.scalar.copy(w_hi[:, half % SPLIT_SLOTS, part, :],
                                   w_raw[:, half % RAW_SLOTS, part, :]).then_inc(hi_ready, 1)
                elif what == "evacuate":
                    kind, place = GROUPS_OF_BANKS[n]
                    act.wait_ge(products_done, LAST_ITEM_OF_GROUP[n] + 1)
                    if kind in ("query", "key"):
                        to = qT if kind == "query" else kT
                        if kind == "key" and n == 1:
                            act.wait_ge(scaled, TILES)
                        for i, bank in enumerate(pair(n)):
                            c = 4 * place + 2 * i
                            last = nc.scalar.copy(to[:, c:c + 2, :], bank[:].rearrange("p (a b) -> p a b", b=SEQ))
                        last.then_inc(act_emptied, 1)
                    elif kind == "value":
                        for t, bank in enumerate(pair(n)):
                            last = nc.scalar.mul(v[:, t, 0:BLOCK], bank[:], 0.5)
                        last.then_inc(act_emptied, 1)
                    elif kind == "value_tile":
                        for c, bank in enumerate(pair(n)):
                            last = nc.scalar.mul(v[:, place, c * BLOCK:(c + 1) * BLOCK], bank[:], 0.5)
                        last.then_inc(act_emptied, 1)
                    elif kind == "gate":
                        if dve_emptied_before(n):
                            act.wait_ge(dve_emptied, dve_emptied_before(n))
                        for t, bank in enumerate(pair(n)):
                            nc.scalar.activation(tanh[:, t, :], bank[:], ACT.Tanh, scale=0.5).then_inc(tanh_ready, 1)
                elif what == "gelu_inner":
                    act.wait_ge(products_done, LAST_ITEM_OF_GROUP[n] + 1)
                    act.wait_ge(dve_emptied, dve_emptied_before(n))
                    for t, bank in enumerate(pair(n)):
                        nc.scalar.activation(y[:, t, 0:BLOCK], bank[:], ACT.Square,
                                             scale=math.sqrt(GELU_C * GELU_A)).then_inc(squared, 1)
                elif what == "gelu_outer":
                    first = TILES * sum(k == "gelu" for k, _ in GROUPS_OF_BANKS[:n])
                    for t in range(TILES):
                        act.wait_ge(inner_ready, first + t + 1)
                        nc.scalar.activation(tanh[:, t, :], y[:, t, 0:BLOCK], ACT.Tanh).then_inc(tanh_ready, 1)
                elif what == "scores":
                    act.wait_ge(masked, n + 1)
                    for t, (a, b) in enumerate(((0, P), (P, 3 * P))):
                        last = nc.scalar.activation(probs[:, n % 2, a:b], probs[:, n % 2, a:b], ACT.Exp,
                                                    scale=-1.0, bias=least[:, n, t:t + 1],
                                                    accum_out=den[:, n, t:t + 1])
                    last.then_inc(probs_ready, 1)
                elif what == "transpose":
                    act.wait_ge(probs_turned, n + 1)
                    if n >= 2:
                        act.wait_ge(values_done, n // 2)
                    nc.scalar.copy(probsT[:, n % 2, :], turn_bank[:, 0:3 * P]).then_inc(probsT_ready, 1)
                elif what == "y_chunk":
                    act.wait_ge(y_turned, n + 1)
                    chunk = y_place(n)[0]
                    nc.scalar.copy(yT_hi[:, chunk, :], y_place(n)[1]).then_inc(y_hi, 1)
                elif what == "ws":
                    act.wait_ge(ws_turned, 1)
                    nc.scalar.copy(wsT, turn_bank[:].rearrange("p (a b) -> p a b", b=P)).then_inc(wsT_ready, 1)
                elif what == "residual":
                    act.wait_ge(added, 2 * n + step[2] + 1)
                    act.wait_ge(squares, 2 * (n + 2) + step[2])
                    square_sum(n + 2, step[2])
                elif what == "hidden":
                    hidden_high(n)
                elif what == "scale" and n >= 2:
                    act.wait_ge(rstd_ready, n + 3)
                    act.wait_ge(with_gain, n + 1)
                    cols = hn[:, n % TILES, BLOCK:D]
                    nc.scalar.mul(cols, cols, rstd[:, n + 2:n + 3]).then_inc(final_act, 1)

        @block.vector
        def _(dve):
            def chain(instruction, semaphore, value):
                instruction.then_inc(semaphore, 1)
                dve.wait_ge(semaphore, value)

            def windows():
                dve.wait_ge(iota_ready, 2)
                nc.vector.tensor_scalar(rel4, rel_i, 3, None, ALU.bitwise_and)
                chain(nc.vector.tensor_scalar(rel16, rel_i, 15, None, ALU.bitwise_and), mask_count, 1)
                nc.vector.tensor_scalar(part_a, rel4, 0.0, None, ALU.is_equal)
                chain(nc.vector.tensor_scalar(part_b, rel16, 0.0, None, ALU.is_equal), mask_count, 2)
                chain(nc.vector.tensor_tensor(n_held, part_a, part_b, ALU.add), mask_count, 3)
                chain(nc.vector.tensor_tensor(n_held, n_held, in_window, ALU.add), mask_count, 4)
                nc.vector.tensor_scalar(part_a, n_held, 2.0, math.log(2.0) / SCALE, ALU.is_equal, ALU.mult)
                nc.vector.tensor_scalar(part_b, n_held, 3.0, math.log(3.0) / SCALE, ALU.is_equal, ALU.mult)
                chain(nc.vector.tensor_scalar(mask_odd[:], n_held, 0.5, MASKED, ALU.is_lt, ALU.mult), mask_count, 5)
                chain(nc.vector.tensor_tensor(mask_odd[:], mask_odd[:], part_a, ALU.add), mask_count, 6)
                nc.vector.tensor_tensor(mask_odd[:], mask_odd[:], part_b, ALU.add).then_inc(mask_built, 1)

            def scale_tile(n, times):
                t = n % TILES
                dve.wait_ge(gain_loaded[n // TILES], 16)
                for c in range(2):
                    cols = slice(c * BLOCK, (c + 1) * BLOCK)
                    last = nc.vector.tensor_tensor(hn[:, t, cols], h[:, t, cols], gain[:, cols], ALU.mult)
                last.then_inc(with_gain, 1)
                dve.wait_ge(with_gain, n - 1)
                dve.wait_ge(rstd_ready, n + 1)
                for c in range(times):
                    cols = slice(c * BLOCK, (c + 1) * BLOCK)
                    nc.vector.tensor_scalar(hn[:, t, cols], hn[:, t, cols], rstd[:, n:n + 1], None,
                                            ALU.mult).then_inc(scaled, 1)

            def hidden_low(n):
                t = n % TILES
                for i, bank in enumerate((score_banks, (turn_bank, value_bank))[t]):
                    dve.wait_ge(hidden_hi, 2 * n + i + 1)
                    place = (slice(None), slice(4 * i, 4 * i + 4), slice(t * P, (t + 1) * P))
                    last = nc.vector.tensor_tensor(hnT_lo[place], bank[:].rearrange("p (a b) -> p a b", b=P),
                                                   hnT_hi[place].bitcast(fp32), ALU.subtract)
                last.then_inc(hidden_ready, 1)

            dve.wait_ge(gain_loaded[0], 16)
            for t in range(TILES):
                dve.wait_ge(x_loaded[t], 16)
                dve.wait_ge(rstd_ready, t + 1)
                for c in range(2):
                    cols = slice(c * BLOCK, (c + 1) * BLOCK)
                    nc.vector.scalar_tensor_tensor(out=hn[:, t, cols], in0=h[:, t, cols], scalar=rstd[:, t:t + 1],
                                                   in1=gain[:, cols], op0=ALU.mult, op1=ALU.mult).then_inc(scaled, 1)
            for step in order:
                what, n = step[0], step[1]
                if what == "rest":
                    half, quarter = n // 2, n % 2
                    dve.wait_ge(hi_ready, n + 1)
                    part = slice(2 * quarter, 2 * quarter + 2)
                    nc.vector.tensor_tensor(w_lo[:, half % SPLIT_SLOTS, part, :], w_raw[:, half % RAW_SLOTS, part, :],
                                            w_hi[:, half % SPLIT_SLOTS, part, :].bitcast(fp32),
                                            ALU.subtract).then_inc(lo_ready, 1)
                elif what == "evacuate" and GROUPS_OF_BANKS[n][0] == "gate":
                    for t, bank in enumerate(pair(n)):
                        dve.wait_ge(tanh_ready, tanh_writes_before(n) + t + 1)
                        last = nc.vector.scalar_tensor_tensor(
                            out=gate[:, GROUPS_OF_BANKS[n][1], t, :], in0=tanh[:, t, :], scalar=1.0, in1=bank[:],
                            op0=ALU.add, op1=ALU.mult)
                    last.then_inc(dve_emptied, 1)
                elif what == "gelu_inner":
                    first = TILES * sum(k == "gelu" for k, _ in GROUPS_OF_BANKS[:n])
                    for t, bank in enumerate(pair(n)):
                        dve.wait_ge(squared, first + t + 1)
                        nc.vector.scalar_tensor_tensor(out=y[:, t, 0:BLOCK], in0=y[:, t, 0:BLOCK], scalar=GELU_C,
                                                       in1=bank[:], op0=ALU.add, op1=ALU.mult
                                                       ).then_inc(inner_ready, 1)
                elif what == "gelu_outer":
                    place = GROUPS_OF_BANKS[n][1] * BLOCK
                    for t, bank in enumerate(pair(n)):
                        dve.wait_ge(tanh_ready, tanh_writes_before(n) + t + 1)
                        last = nc.vector.scalar_tensor_tensor(
                            out=hn[:, t, place:place + BLOCK], in0=tanh[:, t, :], scalar=1.0, in1=bank[:],
                            op0=ALU.add, op1=ALU.mult)
                    last.then_inc(dve_emptied, 1)
                elif what == "layer_norm":
                    vt = hn[:, n, BLOCK:D]
                    dve.wait_ge(dve_emptied, dve_emptied_before(3) + 1)
                    chain(nc.vector.bn_stats(moments[:, n, :], vt), stats, n + 1)
                    nc.vector.bn_aggr(meanvar[:, n, :], moments[:, n, :]).then_inc(stats2, 1)
                    dve.wait_ge(stats2, n + 1)
                    dve.wait_ge(ln_loaded, 32)
                    nc.vector.scalar_tensor_tensor(out=vt, in0=vt, scalar=meanvar[:, n, 0:1], in1=ln_g,
                                                   op0=ALU.subtract, op1=ALU.mult).then_inc(centred, 1)
                    dve.wait_ge(centred, n + 1)
                    dve.wait_ge(ln_plus, 2 * n + 2)
                    nc.vector.scalar_tensor_tensor(out=vt, in0=vt, scalar=rstd[:, 6 + n:7 + n], in1=ln_b,
                                                   op0=ALU.mult, op1=ALU.add).then_inc(v_normed, 1)
                elif what == "mix_u":
                    dve.wait_ge(mix_done, n + 1)
                    dve.wait_ge(bias_loaded, 16)
                    dve.wait_ge(dve_emptied, dve_emptied_before(5) + 1)
                    for g in range(GROUPS):
                        cols = slice(g * P, (g + 1) * P)
                        last = nc.vector.scalar_tensor_tensor(
                            out=y[:, n, cols], in0=score_banks[n][:, cols], scalar=bias_s[:, g:g + 1],
                            in1=hn[:, n, cols], op0=ALU.add, op1=ALU.mult)
                    last.then_inc(mixed, 1)
                elif what == "gating":
                    for t in range(TILES):
                        if n == 1:
                            dve.wait_ge(mixed, TILES)
                            dve.wait_ge(dve_emptied, dve_emptied_before(6) + 1)
                            last = nc.vector.scalar_tensor_tensor(
                                out=y[:, t, 0:BLOCK], in0=y[:, t, 0:BLOCK], scalar=0.25, in1=gate[:, 0, t, :],
                                op0=ALU.mult, op1=ALU.mult)
                        else:
                            c = {0: 1, 2: 0, 3: 1}[n]
                            dve.wait_ge(attended, {0: EVEN_HEADS, 2: EVEN_HEADS + 8, 3: N_HEADS}[n] // 2)
                            dve.wait_ge(dve_emptied, dve_emptied_before({0: 4, 2: 15, 3: 16}[n]) + 1)
                            cols = slice((c if n else 1) * BLOCK, (c + 1 if n else 2) * BLOCK)
                            last = nc.vector.tensor_tensor(y[:, t, cols], y[:, t, cols], gate[:, c, t, :], ALU.mult)
                    last.then_inc(gated, 1)
                elif what == "scores":
                    mask = mask_even if n < EVEN_HEADS else mask_odd
                    dve.wait_ge(scores_done, n + 1)
                    if n == 0:
                        dve.wait_ge(const_pool, 2)
                    if n == EVEN_HEADS:
                        dve.wait_ge(mask_built, 2)
                    if n >= 2:
                        dve.wait_ge(probs_turned, n - 1)
                    for t, (a, b) in enumerate(((0, P), (P, 3 * P))):
                        last = nc.vector.tensor_tensor_reduce(
                            out=probs[:, n % 2, a:b], in0=score_banks[n % 2][:, a:b], in1=mask[:, 2 * P - (b - a):],
                            scale=-SCALE, scalar=3e38, op0=ALU.add, op1=ALU.min, accum_out=least[:, n, t:t + 1])
                    last.then_inc(masked, 1)
                elif what == "values":
                    pair_of = slice(2 * n, 2 * n + 2)
                    dve.wait_ge(values_done, n + 1)
                    chain(nc.vector.reciprocal(rden[:, pair_of, :], den[:, pair_of, :]), inverted, n + 1)
                    column = head_place(2 * n)[2] + (BLOCK if n < EVEN_HEADS // 2 else 0)
                    nc.vector.tensor_tensor(
                        y[:, :, column:column + 2 * HEAD].rearrange("p t (a d) -> p a t d", a=2),
                        value_bank[:, 0:4 * HEAD].rearrange("p (a t d) -> p a t d", a=2, t=TILES),
                        rden[:, pair_of, :].unsqueeze(3).to_broadcast([P, 2, TILES, HEAD]),
                        ALU.mult).then_inc(attended, 1)
                elif what == "y_chunk":
                    chunk, place, _ = y_place(n)
                    dve.wait_ge(y_hi, n + 1)
                    nc.vector.tensor_tensor(yT_lo[:, chunk, :], place, yT_hi[:, chunk, :].bitcast(fp32),
                                            ALU.subtract).then_inc(y_lo, 1)
                elif what == "residual":
                    layer, t, c = n // TILES, n % TILES, step[2]
                    group = (7, 17)[layer] + t
                    dve.wait_ge(products_done, LAST_ITEM_OF_GROUP[group] + 1 - 2 * (1 - c))
                    cols = slice(c * BLOCK, (c + 1) * BLOCK)
                    nc.vector.tensor_tensor(h[:, t, cols], h[:, t, cols], pair(group)[c][:],
                                            ALU.add).then_inc(added, 1)
                elif what == "windows":
                    windows()
                elif what == "scale":
                    dve.wait_ge(added, 2 * n + 2)
                    scale_tile(2 + n, 2 if n < TILES else 1)
                elif what == "hidden":
                    hidden_low(n)

        @block.tensor
        def _(pe):
            def turn(to, of):
                return nc.tensor.matmul(to, of, ident[:], is_transpose=True, start=True, stop=True)

            def hidden_turn(n):
                t = n % TILES
                for i, bank in enumerate((score_banks, (turn_bank, value_bank))[t]):
                    pe.wait_ge(scaled, 2 * n + i + 1)
                    for c in range(4):
                        last = turn(bank[:, c * P:(c + 1) * P], hn[:, t, (4 * i + c) * P:(4 * i + c + 1) * P])
                    last.then_inc(hidden_turned, 1)

            pe.wait_ge(const_pool, 2)
            started = set()
            pairs_valued = chunks_turned = 0
            for step in order:
                what, n = step[0], step[1]
                if what == "product":
                    half_item = step[2]
                    group, half, quarter, side = ITEMS[n]
                    kind, place = GROUPS_OF_BANKS[group]
                    matrix, chunk0, _ = HALVES[half]
                    if half_item == 0:
                        if n == 0:
                            pe.wait_ge(hidden_ready, TILES)
                        pe.wait_ge(lo_ready, 2 * half + quarter + 1)
                        if group >= 2 and group not in started:
                            wait_emptied(pe, group - 2)
                        started.add(group)
                        if kind == "residual":
                            layer = 0 if matrix == "even_out" else 1
                            first = chunk0 + 2 * quarter
                            order_of = {c: i for i, c in enumerate((4, 5, 6, 7, 0, 1, 2, 3) if layer == 0
                                                                   else range(CHUNKS))}
                            pe.wait_ge(y_lo, CHUNKS * layer + max(order_of[first], order_of[first + 1]) + 1)
                        if kind == "value_tile":
                            pe.wait_ge(hidden_ready, TILES + place + 1)
                    hi, lo = (yT_hi, yT_lo) if kind == "residual" else (hnT_hi, hnT_lo)
                    r = 2 * quarter + half_item
                    chunk = chunk0 + r
                    slot = half % SPLIT_SLOTS
                    begins = chunk == (HALF_CHUNKS if matrix == "even_out" else 0)
                    ends = chunk == (HALF_CHUNKS - 1 if matrix == "even_out" else CHUNKS - 1)
                    if kind in ("query", "key"):
                        for c in range(4):
                            to = pair(group)[c // 2][:, (c % 2) * SEQ:(c % 2 + 1) * SEQ]
                            cols = slice(c * P, (c + 1) * P)
                            wh, wl = w_hi[:, slot, r, cols], w_lo[:, slot, r, cols]
                            nc.tensor.matmul(to, wh, hi[:, chunk, :], start=begins and c % 2 == 0, stop=False,
                                             skip_group_check=True)
                            nc.tensor.matmul(to, wh, lo[:, chunk, :], start=False, stop=False,
                                             skip_group_check=True)
                            last = nc.tensor.matmul(to, wl, hi[:, chunk, :], start=False, stop=ends,
                                                    skip_group_check=True)
                    else:
                        if side is None:
                            targets = [(t, pair(group)[t]) for t in range(TILES)]
                        else:
                            targets = [(place, pair(group)[side])]
                        for t, to in targets:
                            rows = slice(t * P, (t + 1) * P)
                            xh, xl = hi[:, chunk, rows], lo[:, chunk, rows]
                            nc.tensor.matmul(to[:], xh, w_hi[:, slot, r, :], start=begins, stop=False)
                            nc.tensor.matmul(to[:], xl, w_hi[:, slot, r, :], start=False, stop=False)
                            last = nc.tensor.matmul(to[:], xh, w_lo[:, slot, r, :], start=False, stop=ends)
                    if half_item == 1:
                        last.then_inc(products_done, 1)
                elif what == "scores":
                    chunk, row, _ = head_place(n)
                    if n == 0:
                        pe.wait_ge(act_emptied, 2)
                    elif n in (EVEN_HEADS, EVEN_HEADS + 8):
                        pe.wait_ge(act_emptied, count_of_kind(ACT_KINDS, 12 if n == EVEN_HEADS else 14))
                    if n >= 2:
                        pe.wait_ge(masked, n - 1)
                    q, k = qT[row:row + HEAD, chunk, :], kT[row:row + HEAD, chunk, :]
                    bank = score_banks[n % 2]
                    nc.tensor.matmul(bank[:, 0:P], q[:, 0:P], k[:, 0:P], start=True, stop=True)
                    nc.tensor.matmul(bank[:, P:3 * P], q[:, P:SEQ], k, start=True, stop=True).then_inc(scores_done, 1)
                elif what == "transpose":
                    pe.wait_ge(probs_ready, n + 1)
                    if n >= 1:
                        pe.wait_ge(probsT_ready, n)
                    for i in range(3):
                        last = turn(turn_bank[:, i * P:(i + 1) * P], probs[:, n % 2, i * P:(i + 1) * P])
                    last.then_inc(probs_turned, 1)
                elif what == "values":
                    pe.wait_ge(probsT_ready, 2 * n + 2)
                    if n >= 1:
                        pe.wait_ge(attended, n)
                    if chunks_turned:
                        pe.wait_ge(y_lo, chunks_turned)
                    pairs_valued = n + 1
                    for a in range(2):
                        column = head_place(2 * n + a)[2]
                        pT = probsT[:, a, :]
                        v0, v1 = v[:, 0, column:column + HEAD], v[:, 1, column:column + HEAD]
                        first, second = (value_bank[:, (2 * a + t) * HEAD:(2 * a + t + 1) * HEAD] for t in range(2))
                        nc.tensor.matmul(first, pT[:, 0:P], v0, start=True, stop=True)
                        nc.tensor.matmul(second, pT[:, P:2 * P], v0, start=True, stop=False)
                        last = nc.tensor.matmul(second, pT[:, 2 * P:3 * P], v1, start=False, stop=True)
                    last.then_inc(values_done, 1)
                elif what == "mix":
                    pe.wait_ge(wsT_ready, 1)
                    pe.wait_ge(v_normed, n + 1)
                    pe.wait_ge(masked, EVEN_HEADS)
                    for g in range(GROUPS):
                        cols = slice(BLOCK + g * P, BLOCK + (g + 1) * P)
                        last = nc.tensor.matmul(score_banks[n][:, g * P:(g + 1) * P], wsT[:, g, :], hn[:, n, cols],
                                                start=True, stop=True)
                    last.then_inc(mix_done, 1)
                elif what == "y_chunk":
                    chunk, place, alone = y_place(n)
                    pe.wait_ge(gated, n // 4 + 1)
                    before = n - 1 if alone else n - 2
                    if n % 4 == 0:
                        before = n - 1
                    if before >= 0:
                        pe.wait_ge(y_lo, before + 1)
                    pe.wait_ge(attended, pairs_valued)
                    chunks_turned = n + 1
                    if n % 4 == 1:
                        pe.wait_ge(probsT_ready, {1: EVEN_HEADS, 5: EVEN_HEADS, 9: EVEN_HEADS, 13: N_HEADS}[n])
                    for t in range(TILES):
                        last = turn(place[:, t * P:(t + 1) * P], y[:, t, chunk * P:(chunk + 1) * P])
                    last.then_inc(y_turned, 1)
                elif what == "ws":
                    pe.wait_ge(ws_masked, 1)
                    for g in range(GROUPS):
                        last = turn(turn_bank[:, g * P:(g + 1) * P], ws[:, g, :])
                    last.then_inc(ws_turned, 1)
                elif what == "hidden":
                    if n == 2:
                        pe.wait_ge(mixed, TILES)
                    hidden_turn(n)


_NAMES = ("x", "norm_g", "final_norm_g", "ab_w_in", "ab_w_out", "gmlp_ln_g", "gmlp_ln_b", "gmlp_w_s", "gmlp_b_s",
          "c_w_in", "c_w_out")


def kernel(**inputs):
    import numpy as np
    import concourse.bacc as bacc
    from concourse.bass_utils import run_bass_kernel_spmd

    nc = bacc.Bacc("TRN2", target_bir_lowering=False, num_devices=1)
    arrays, args = {}, []
    for name in _NAMES:
        a = np.ascontiguousarray(inputs[name])
        arrays[f"in_{name}"] = a
        args.append(nc.dram_tensor(f"in_{name}", a.shape, mybir.dt.from_np(a.dtype), kind="ExternalInput").ap())
    out = nc.dram_tensor("out_0", (1, SEQ, D), mybir.dt.float32, kind="ExternalOutput").ap()
    build(nc, *args, out)
    result = run_bass_kernel_spmd(nc, [arrays], core_ids=[0])
    return result.results[0]["out_0"]
```

```python
import math
from contextlib import ExitStack

import concourse.bass as bass
from concourse import mybir
from concourse.alu_op_type import AluOpType as ALU

P = 128
SEQ = 256
TILES = SEQ // P
D = 1024
CHUNKS = D // P
BLOCK = 512
HALF_CHUNKS = CHUNKS // 2
HEAD = 64
EVEN_HEADS = 8
ODD_HEADS = 16
HEADS_OF_SET = 8
GROUPS = 4
EPS = 1e-6
SCALE = HEAD ** -0.5
MASKED = -1e30
GELU_C = math.sqrt(2.0 / math.pi)
GELU_A = 0.044715
RAW_SLOTS = 3
SPLIT_SLOTS = 9

SOON, AHEAD, RATE, MOST_TURNS, LAG = 4, 13, 2.0, 5.0, 2

HEADS_AT = (
    ((10, 14, 19, 23),
     (6, 9, 10, 12, 14, 17, 19, 21),
     (3, 3, 6, 9, 10, 12, 13, 17)),
    ((9, 13, 15, 20),
     (5, 7, 9, 10, 13, 14, 15, 18),
     (3, 4, 6, 7, 10, 10, 13, 14)),
    ((8, 11, 14, 21),
     (4, 5, 8, 9, 11, 12, 14, 17),
     (3, 3, 4, 4, 9, 9, 13, 14)),
)
EVEN_AT = (
    (8, ("gelu_inner", 4)), (9, ("gelu_outer", 4)), (10, ("layer_norm", 0)), (13, ("layer_norm", 1)),
    (20, ("mix", 0)), (26, ("mix", 1)), (24, ("gating", 0)), (29, ("y_pair", 0)), (29, ("y_pair", 1)),
    (25, ("gelu_inner", 6)), (27, ("gelu_outer", 6)), (27, ("mix_u", 0)), (30, ("mix_u", 1)),
    (37, ("gating", 1)), (43, ("y_pair", 2)), (44, ("y_pair", 3)),
)
NORM_AT = (
    (-13, ("residual", 0, 0)), (-10, ("residual", 0, 1)), (-6, ("scale", 0)), (-3, ("hidden", 2)),
    (-2, ("residual", 1, 0)), (4, ("residual", 1, 1)), (5, ("scale", 1)), (12, ("hidden", 3)),
)
ODD_AT = (
    (1, ("gating", 2)), (4, ("y_pair", 4)), (7, ("y_pair", 5)), (19, ("gating", 3)), (21, ("y_pair", 6)),
    (22, ("y_pair", 7)),
)
END_AT = (
    (12, ("residual", 2, 0)), (11, ("residual", 2, 1)), (7, ("scale", 2)), (9, ("residual", 3, 0)),
)
HIDDEN_1_AT, WINDOWS_AT, WS_AT = (5, 10, -2)
KEYS_AGAIN_AT = (5, 6, 5)
KEYS_AGAIN_BY = ("act", "dve")
WARM = (6, 4, 10)


def plan():
    halves, groups, items = [], [], []

    def whole(matrix, column, kind, place):
        g = len(groups)
        groups.append((kind, place))
        for part in range(2):
            h = len(halves)
            halves.append((matrix, part * HALF_CHUNKS, column))
            items.extend((g, h, q, None) for q in range(2))

    def output(matrix, parts):
        g = len(groups)
        groups.extend([("residual", 0), ("residual", 1)])
        for part in parts:
            h = len(halves)
            halves.extend((matrix, part * HALF_CHUNKS, c * BLOCK) for c in range(2))
            for tile in range(TILES):
                items.extend((g + tile, h + c, q, c) for c in range(2) for q in range(2))

    u, v, ga, q, k, vv, gb = (i * BLOCK for i in range(7))
    groups.extend([("value_half", 0), ("value_half", 1)])
    halves.extend(("even_in", part * HALF_CHUNKS, vv) for part in range(2))
    for tile in range(TILES):
        items.extend((tile, i, q_, 0) for i in range(2) for q_ in range(2))
    whole("even_in", q, "query", 0)
    whole("even_in", k, "key", 0)
    whole("even_in", v, "gelu", 1)
    whole("even_in", gb, "gate", 1)
    whole("even_in", u, "gelu", 0)
    whole("even_in", ga, "gate", 0)
    output("even_out", (1, 0))
    g, h = len(groups), len(halves)
    groups.extend([("value_tile", 0), ("value_tile", 1)])
    halves.extend(("odd_in", part * HALF_CHUNKS, 2 * D + c * BLOCK) for c in range(2) for part in range(2))
    for tile in range(TILES):
        items.extend((g + tile, h + i, q, i // 2) for i in range(4) for q in range(2))
    for c in range(2):
        whole("odd_in", c * BLOCK, "query", c)
        whole("odd_in", D + c * BLOCK, "key", c)
    for c in range(2):
        whole("odd_in", 3 * D + c * BLOCK, "gate", c)
    output("odd_out", (0, 1))
    return halves, groups, items


HALVES, GROUPS_OF_BANKS, ITEMS = plan()
LAST_ITEM_OF_GROUP = {item[0]: n for n, item in enumerate(ITEMS)}
LAST_ITEM_OF_QUARTER = {2 * item[1] + item[2]: n for n, item in enumerate(ITEMS)}
VALUE_KINDS = ("value_half", "value_tile")
SPLIT_KINDS = ("query", "key")


def steps():
    out = [("round", 0), ("rest", 0), ("hidden", 0), ("round", 1), ("rest", 1), ("round", 2), ("rest", 2),
           ("squares", 1), ("round", 3), ("norm", 1), ("rest", 3)]
    split = 4
    first_item = {}
    for n, item in enumerate(ITEMS):
        first_item.setdefault(item[0], n)
    extra = {}

    def at(position, *what):
        extra.setdefault(position, []).extend(what)

    def heads(heads_set, start):
        for stage, places in zip(("values", "transpose", "scores"), HEADS_AT[heads_set]):
            for n, place in enumerate(places):
                at(start + place, (stage, heads_set * len(places) + n))

    at(HIDDEN_1_AT, ("hidden", 1))
    at(2 * first_item[2] + WINDOWS_AT, ("windows", 0))
    even = 2 * first_item[4]
    at(even + WS_AT, ("ws", 0))
    heads(0, even)
    for place, step in EVEN_AT:
        at(even + place, step)
    odd = 2 * first_item[10]
    for place, step in NORM_AT:
        at(odd + place, step)
    for last_keys, place in zip((3, 13, 15), KEYS_AGAIN_AT):
        at(2 * first_item[last_keys + 1] + place, ("again", last_keys, 1))
    heads(1, 2 * first_item[14])
    heads(2, 2 * first_item[16])
    for place, step in ODD_AT:
        at(2 * first_item[17] + place, step)

    end = 2 * len(ITEMS)
    for place, step in END_AT:
        at(end - place, step)

    first_use = {}
    for n, item in enumerate(ITEMS):
        first_use.setdefault(2 * item[1] + item[2], n)
    freed, turns, rounded = {}, 0.0, []
    for n, item in enumerate(ITEMS):
        turns = min(turns + (RATE if item[3] is None else RATE / 2), MOST_TURNS)
        for half in range(2):
            while half == 0 and n >= 4 and split < 2 * len(HALVES):
                soon = first_use[split] <= n + SOON
                before = split - SPLIT_SLOTS
                if before >= 0 and freed.get(before, n) > n - 1:
                    break
                if not soon and (turns < 1.0 or first_use[split] > n + AHEAD):
                    break
                out.append(("round", split))
                rounded.append(split)
                split += 1
                turns = max(turns - 1.0, -1.0)
            while rounded and (len(rounded) > LAG or first_use[rounded[0]] <= n + 1):
                out.append(("rest", rounded.pop(0)))
            out.extend(extra.pop(2 * n + half, ()))
            out.append(("product", n, half))
        if LAST_ITEM_OF_QUARTER[2 * item[1] + item[2]] == n:
            freed[2 * item[1] + item[2]] = n
        g = item[0]
        if LAST_ITEM_OF_GROUP[g] == n and GROUPS_OF_BANKS[g][0] not in ("gelu", "residual"):
            out.append(("evacuate", g))
            if GROUPS_OF_BANKS[g][0] == "key":
                out.append(("again", g, 0))
    assert not extra, extra
    out.extend([("residual", 3, 1), ("scale", 3)])
    return out


def count_of_kind(kinds, group):
    return sum(k in kinds for k, _ in GROUPS_OF_BANKS[: group + 1])


def build(nc, x, norm_g, final_norm_g, ab_w_in, ab_w_out, gmlp_ln_g, gmlp_ln_b, gmlp_w_s, gmlp_b_s,
          c_w_in, c_w_out, out):
    fp32 = mybir.dt.float32
    fp32r = mybir.dt.float32r
    int32 = mybir.dt.int32
    ACT = mybir.ActivationFunctionType
    matrices = {"even_in": ab_w_in[0], "even_out": ab_w_out[0], "odd_in": c_w_in[0], "odd_out": c_w_out[0]}
    order = steps()
    x_tiles = x[0].rearrange("(t p) c -> t p c", p=P)
    out_tiles = out[0].rearrange("(t p) c -> t p c", p=P)
    N_HEADS = EVEN_HEADS + ODD_HEADS

    ctx = ExitStack()
    with ctx:
        def sb(name, shape, dtype=fp32):
            return ctx.enter_context(nc.sbuf_tensor(name, shape, dtype))

        def sem(name):
            return ctx.enter_context(nc.semaphore(name))

        ctx.enter_context(nc.allow_non_contiguous_dma(reason="a bias of 512 numbers, once"))
        w_raw = sb("w_raw", [P, RAW_SLOTS, HALF_CHUNKS, BLOCK])
        w_hi = sb("w_hi", [P, SPLIT_SLOTS, HALF_CHUNKS // 2, BLOCK], fp32r)
        w_lo = sb("w_lo", [P, SPLIT_SLOTS, HALF_CHUNKS // 2, BLOCK], fp32r)
        h = sb("h", [P, TILES, D])
        hn = sb("hn", [P, TILES, D])
        hnT_hi = sb("hnT_hi", [P, CHUNKS, SEQ], fp32r)
        hnT_lo = sb("hnT_lo", [P, CHUNKS, SEQ], fp32r)
        yT_hi = sb("yT_hi", [P, CHUNKS, SEQ], fp32r)
        yT_lo = sb("yT_lo", [P, CHUNKS, SEQ], fp32r)
        q_own = sb("q_own", [P, HEADS_OF_SET, SEQ], fp32r)
        k_own = sb("k_own", [P, HEADS_OF_SET, SEQ], fp32r)
        k_low = sb("k_low", [P, 2, HEADS_OF_SET // 2, SEQ], fp32r)
        v = sb("v", [P, TILES, D])
        gate = sb("gate", [P, 2, TILES, BLOCK])
        y = sb("y", [P, TILES, D])
        tanh = sb("tanh", [P, TILES, BLOCK])
        probs = sb("probs", [P, 2, 3 * P])
        probsT = sb("probsT", [P, 2, 3 * P])
        least = sb("least", [P, N_HEADS, 2])
        den = sb("den", [P, N_HEADS, 2])
        rden = sb("rden", [P, N_HEADS, 2])
        mask_even = sb("mask_even", [P, 2 * P])
        mask_odd = sb("mask_odd", [P, 2 * P])
        ident = sb("ident", [P, P])
        bias_s = sb("bias_s", [P, GROUPS])
        sumsq = sb("sumsq", [P, 6, 2])
        rstd = sb("rstd", [P, 8])
        power = sb("power", [P, 1])
        gain_rows = sb("gain_rows", [2 * CHUNKS, P])
        gain_of = sb("gain_of", [P, 2 * CHUNKS])
        moments = sb("moments", [P, TILES, nc.vector.BN_STATS_DIM])
        meanvar = sb("meanvar", [P, TILES, nc.vector.BN_AGGR_DIM])
        gain = gate[:, 0, :, :].rearrange("p a b -> p (a b)")
        ws = tanh[:, 0, :].rearrange("p (b s) -> p b s", s=P)
        wsT = hn[:, 0, 0:BLOCK].rearrange("p (b t) -> p b t", t=P)
        q_stack = (yT_hi, yT_hi, q_own)
        k_twice = (yT_lo, yT_lo, k_own)
        k_rest = (k_low[:, 0], k_low[:, 0], k_low[:, 1])
        ln_g, ln_b = v[:, 0, BLOCK:D], v[:, 1, BLOCK:D]
        rel4 = gate[:, 0, 0, 0:2 * P].bitcast(int32)
        rel16 = gate[:, 0, 0, 2 * P:4 * P].bitcast(int32)
        rel_i = gate[:, 1, 0, 0:2 * P].bitcast(int32)
        n_held = gate[:, 1, 1, 0:2 * P]
        part_a = gate[:, 0, 1, 0:2 * P]
        part_b = gate[:, 0, 1, 2 * P:4 * P]
        in_window = gate[:, 1, 1, 2 * P:4 * P]

        banks = [ctx.enter_context(nc.psum_tensor(f"products{i}", [P, BLOCK], fp32)) for i in range(4)]
        score_banks = [ctx.enter_context(nc.psum_tensor(f"scores{i}", [P, BLOCK], fp32)) for i in range(2)]
        turn_bank = ctx.enter_context(nc.psum_tensor("turned", [P, BLOCK], fp32))
        value_bank = ctx.enter_context(nc.psum_tensor("attended", [P, BLOCK], fp32))

        w_loaded = [sem(f"w_loaded{i}") for i in range(RAW_SLOTS)]
        x_loaded = [sem(f"x_loaded{i}") for i in range(TILES)]
        gains_loaded, gains_turned, gains_ready = sem("gains_loaded"), sem("gains_turned"), sem("gains_ready")
        final_gain_loaded = sem("final_gain_loaded")
        ws_loaded, ln_loaded, bias_loaded = sem("ws_loaded"), sem("ln_loaded"), sem("bias_loaded")
        stored = sem("stored")
        hi_ready, lo_ready = sem("hi_ready"), sem("lo_ready")
        products_done = sem("products_done")
        act_emptied, dve_emptied = sem("act_emptied"), sem("dve_emptied")
        heads_high, heads_low = sem("heads_high"), sem("heads_low")
        keys_twice = [sem(f"keys_twice{i}") for i in range(2)]
        const_pool = sem("const_pool")
        iota_ready, mask_count = sem("iota_ready"), sem("mask_count")
        mask_built = sem("mask_built")
        ws_masked, ws_turned, wsT_ready = sem("ws_masked"), sem("ws_turned"), sem("wsT_ready")
        squares_dve = sem("squares_dve")
        squares, with_eps, rstd_ready = sem("squares"), sem("with_eps"), sem("rstd_ready")
        with_gain, final_act = sem("with_gain"), sem("final_act")
        first_scaled = sem("first_scaled")
        w_first = [sem(f"w_first{i}") for i in range(2)]
        added, scaled = sem("added"), sem("scaled")
        hidden_turned, hidden_hi, hidden_ready = sem("hidden_turned"), sem("hidden_hi"), sem("hidden_ready")
        scores_done, masked, probs_ready = sem("scores_done"), sem("masked"), sem("probs_ready")
        probs_turned, probsT_ready = sem("probs_turned"), sem("probsT_ready")
        values_done, inverted, attended = sem("values_done"), sem("inverted"), sem("attended")
        squared, inner_ready = sem("squared"), sem("inner_ready")
        tanh_ready = sem("tanh_ready")
        stats, stats2, centred, v_normed = sem("stats"), sem("stats2"), sem("centred"), sem("v_normed")
        ln_plus = sem("ln_plus")
        mix_done, mixed = sem("mix_done"), sem("mixed")
        gated = sem("gated")
        y_turned, y_hi, y_lo = sem("y_turned"), sem("y_hi"), sem("y_lo")

        def pair(group):
            return banks[2 * (group % 2)], banks[2 * (group % 2) + 1]

        def wait_emptied(engine, group):
            if GROUPS_OF_BANKS[group][0] in VALUE_KINDS:
                engine.wait_ge(act_emptied, count_of_kind(VALUE_KINDS, group))
            elif GROUPS_OF_BANKS[group][0] in SPLIT_KINDS:
                engine.wait_ge(heads_low, 2 * count_of_kind(SPLIT_KINDS, group))
            elif GROUPS_OF_BANKS[group][0] == "residual":
                engine.wait_ge(added, 2 * count_of_kind(("residual",), group))
            else:
                engine.wait_ge(dve_emptied, count_of_kind(("gate", "gelu"), group))

        def dve_emptied_before(group):
            return count_of_kind(("gate", "gelu"), group - 1)

        def tanh_writes_before(group):
            return TILES * dve_emptied_before(group)

        def value_column(head):
            return HEAD * (head if head < EVEN_HEADS else head - EVEN_HEADS)

        def rows_of(side):
            return slice(side * HEAD, (side + 1) * HEAD)

        def set_of_heads(group):
            return count_of_kind(SPLIT_KINDS, group - 1) // 2

        def heads_of(bank, side):
            return slice(4 * bank + side, 4 * bank + side + 3, 2)

        def y_place(n):
            first = (4, 6, 0, 2)[n] if n < HALF_CHUNKS else 2 * (n - HALF_CHUNKS)
            return first, (turn_bank if n in (1, 3, 7) else value_bank)

        def keys_again(engine, copy, group, i):
            heads_set = set_of_heads(group)
            to = k_twice[heads_set]
            engine.wait_ge(heads_high, 2 * count_of_kind(SPLIT_KINDS, group - 1) + i + 1)
            for side in range(2):
                last = copy(to[rows_of(1 - side), heads_of(i, side), :],
                            to[rows_of(side), heads_of(i, side), :].bitcast(fp32))
            last.then_inc(keys_twice[i], 1)

        block = ctx.enter_context(nc.Block())

        @block.sync
        def _(sp):
            sp.dma_start(h[:, 0, :], x_tiles[0]).then_inc(x_loaded[0], 16)
            sp.dma_start(gain_rows[:], norm_g.rearrange("l (c p) -> (l c) p", p=P)).then_inc(gains_loaded, 16)
            for n, (matrix, chunk, column) in enumerate(HALVES):
                if n >= RAW_SLOTS:
                    sp.wait_ge(lo_ready, 2 * (n - RAW_SLOTS + 1))
                rows = matrices[matrix][chunk * P:(chunk + HALF_CHUNKS) * P, column:column + BLOCK]
                rows = rows.rearrange("(k p) c -> p k c", p=P)
                if n < 2:
                    sp.dma_start(w_raw[:, n, 0:2], rows[:, 0:2]).then_inc(w_first[n], 16)
                    if n == 1:
                        sp.dma_start(h[:, 1, :], x_tiles[1]).then_inc(x_loaded[1], 16)
                    sp.dma_start(w_raw[:, n, 2:4], rows[:, 2:4]).then_inc(w_loaded[n], 16)
                    continue
                sp.dma_start(w_raw[:, n % RAW_SLOTS], rows).then_inc(w_loaded[n % RAW_SLOTS], 16)
                if n == 2:
                    sp.wait_ge(squares, 3)
                    sp.dma_start(ws, gmlp_w_s[0].rearrange("g t s -> t g s")).then_inc(ws_loaded, 16)
                    sp.dma_start(ln_g, gmlp_ln_g.partition_broadcast(P)).then_inc(ln_loaded, 16)
                    sp.dma_start(ln_b, gmlp_ln_b.partition_broadcast(P)).then_inc(ln_loaded, 16)
                    sp.dma_start(bias_s[:], gmlp_b_s[0].rearrange("g t -> t g")).then_inc(bias_loaded, 16)
            for t in range(TILES):
                sp.wait_ge(scaled, 2 * (2 * TILES - 1) + t + 1)
                sp.dma_start(out_tiles[t][:, 0:BLOCK], hn[:, t, 0:BLOCK]).then_inc(stored, 16)
                sp.wait_ge(final_act, t + 1)
                sp.dma_start(out_tiles[t][:, BLOCK:D], hn[:, t, BLOCK:D]).then_inc(stored, 16)
            sp.wait_ge(stored, 16 * 2 * TILES)

        @block.gpsimd
        def _(pool):
            nc.gpsimd.memset(power[:], -0.5)
            nc.gpsimd.memset(ident[:], 0.0)
            nc.gpsimd.memset(mask_even[:], 0.0).then_inc(const_pool, 1)
            pool.wait_ge(const_pool, 1)
            nc.gpsimd.affine_select(out=ident[:], in_=ident[:], compare_op=ALU.not_equal, fill=1.0,
                                    base=0, pattern=[[-1, P]], channel_multiplier=1)
            nc.gpsimd.affine_select(out=mask_even[:, P:], in_=mask_even[:, P:], compare_op=ALU.is_ge,
                                    fill=MASKED, base=0, pattern=[[-1, P]],
                                    channel_multiplier=1).then_inc(const_pool, 1)
            nc.gpsimd.iota(rel_i, pattern=[[-1, 2 * P]], base=P + SEQ, channel_multiplier=1)
            nc.gpsimd.memset(in_window, 1.0).then_inc(iota_ready, 1)
            pool.wait_ge(iota_ready, 1)
            nc.gpsimd.affine_select(out=in_window, in_=in_window, compare_op=ALU.is_ge, fill=0.0, base=0,
                                    pattern=[[1, 2 * P]], channel_multiplier=-1).then_inc(iota_ready, 1)

            def root_of_squares(n):
                first, second = sumsq[:, n, 0:1], sumsq[:, n, 1:2]
                pool.wait_ge(squares, 1 if n == 0 else 2 * n)
                nc.gpsimd.tensor_scalar(first, first, EPS, None, ALU.add).then_inc(with_eps, 1)
                if n == 0:
                    pool.wait_ge(squares_dve, 1)
                else:
                    pool.wait_ge(squares, 2 * n + 1)
                pool.wait_ge(with_eps, 2 * n + 1)
                nc.gpsimd.tensor_tensor(first, first, second, ALU.add).then_inc(with_eps, 1)
                pool.wait_ge(with_eps, 2 * n + 2)
                nc.gpsimd.tensor_tensor(rstd[:, n:n + 1], first, power[:], ALU.pow).then_inc(rstd_ready, 1)

            root_of_squares(0)
            root_of_squares(1)
            pool.wait_ge(ws_loaded, 16)
            nc.gpsimd.affine_select(out=ws, in_=ws, compare_op=ALU.is_ge, fill=0.0, base=0,
                                    pattern=[[0, GROUPS], [-1, P]], channel_multiplier=1).then_inc(ws_masked, 1)
            pool.wait_ge(mask_built, 1)
            nc.gpsimd.affine_select(out=mask_odd[:], in_=mask_odd[:], compare_op=ALU.is_ge, fill=MASKED,
                                    base=P, pattern=[[-1, 2 * P]], channel_multiplier=1).then_inc(mask_built, 1)
            for t in range(TILES):
                pool.wait_ge(stats2, t + 1)
                nc.gpsimd.tensor_scalar(meanvar[:, t, 1:2], meanvar[:, t, 1:2], 1.0, 4 * EPS, ALU.mult,
                                        ALU.add).then_inc(ln_plus, 1)
                pool.wait_ge(ln_plus, 2 * t + 1)
                nc.gpsimd.tensor_tensor(rstd[:, 6 + t:7 + t], meanvar[:, t, 1:2], power[:],
                                        ALU.pow).then_inc(ln_plus, 1)
            root_of_squares(2)
            root_of_squares(3)
            pool.wait_ge(gated, 3)
            pool.dma_start(gain, final_norm_g[None, :].partition_broadcast(P)).then_inc(final_gain_loaded, 16)
            root_of_squares(4)
            root_of_squares(5)

        @block.scalar
        def _(act):
            act.wait_ge(const_pool, 1)
            nc.scalar.activation(rstd[:, 0:1], power[:], ACT.Tanh)

            def square_sum(n, c):
                t = n % TILES
                nc.scalar.activation(tanh[:, t, :], h[:, t, c * BLOCK:(c + 1) * BLOCK], ACT.Square,
                                     scale=D ** -0.5, accum_out=sumsq[:, n, c:c + 1]).then_inc(squares, 1)

            def hidden_high(n):
                t = n % TILES
                for i, bank in enumerate((score_banks, (turn_bank, value_bank))[t]):
                    act.wait_ge(hidden_turned, 2 * n + i + 1)
                    for c in range(4):
                        gain_col = CHUNKS * (n // TILES) + 4 * i + c
                        last = nc.scalar.mul(hnT_hi[:, 4 * i + c, t * P:(t + 1) * P], bank[:, c * P:(c + 1) * P],
                                             gain_of[:, gain_col:gain_col + 1])
                    last.then_inc(hidden_hi, 1)

            act.wait_ge(x_loaded[0], 16)
            square_sum(0, 0)
            act.wait_ge(gains_turned, 1)
            nc.scalar.copy(gain_of[:], turn_bank[:, 0:2 * CHUNKS]).then_inc(gains_ready, 1)
            act.wait_ge(gains_ready, 1)
            for step in order:
                what, n = step[0], step[1]
                if what == "squares":
                    act.wait_ge(x_loaded[1], 16)
                    square_sum(1, 0)
                    act.wait_ge(squares, 2)
                    square_sum(1, 1)
                elif what == "round":
                    half, quarter = n // 2, n % 2
                    if n in (0, 2):
                        act.wait_ge(w_first[half], 16)
                    else:
                        act.wait_ge(w_loaded[half % RAW_SLOTS], 16 * (half // RAW_SLOTS + 1))
                    if n >= SPLIT_SLOTS:
                        act.wait_ge(products_done, LAST_ITEM_OF_QUARTER[n - SPLIT_SLOTS] + 1)
                    part = slice(2 * quarter, 2 * quarter + 2)
                    nc.scalar.copy(w_hi[:, n % SPLIT_SLOTS, :, :],
                                   w_raw[:, half % RAW_SLOTS, part, :]).then_inc(hi_ready, 1)
                elif what == "evacuate":
                    kind, place = GROUPS_OF_BANKS[n]
                    act.wait_ge(products_done, LAST_ITEM_OF_GROUP[n] + 1)
                    if kind in SPLIT_KINDS:
                        to = (q_stack if kind == "query" else k_twice)[set_of_heads(n)]
                        for i, bank in enumerate(pair(n)):
                            for side in range(2):
                                rows = rows_of(side)
                                last = nc.scalar.copy(to[rows, heads_of(i, side), :],
                                                      bank[rows, :].rearrange("p (a b) -> p a b", b=SEQ))
                            last.then_inc(heads_high, 1)
                    elif kind == "value_half":
                        nc.scalar.mul(v[:, place, 0:BLOCK], pair(n)[0][:], 0.5).then_inc(act_emptied, 1)
                    elif kind == "value_tile":
                        for c, bank in enumerate(pair(n)):
                            last = nc.scalar.mul(v[:, place, c * BLOCK:(c + 1) * BLOCK], bank[:], 0.5)
                        last.then_inc(act_emptied, 1)
                    elif kind == "gate":
                        if dve_emptied_before(n):
                            act.wait_ge(dve_emptied, dve_emptied_before(n))
                        for t, bank in enumerate(pair(n)):
                            nc.scalar.activation(tanh[:, t, :], bank[:], ACT.Tanh, scale=0.5).then_inc(tanh_ready, 1)
                elif what == "again" and KEYS_AGAIN_BY[step[2]] == "act":
                    keys_again(act, nc.scalar.copy, n, step[2])
                elif what == "gelu_inner":
                    act.wait_ge(products_done, LAST_ITEM_OF_GROUP[n] + 1)
                    act.wait_ge(dve_emptied, dve_emptied_before(n))
                    for t, bank in enumerate(pair(n)):
                        nc.scalar.activation(y[:, t, 0:BLOCK], bank[:], ACT.Square,
                                             scale=math.sqrt(GELU_C * GELU_A)).then_inc(squared, 1)
                elif what == "gelu_outer":
                    first = TILES * sum(k == "gelu" for k, _ in GROUPS_OF_BANKS[:n])
                    for t in range(TILES):
                        act.wait_ge(inner_ready, first + t + 1)
                        nc.scalar.activation(tanh[:, t, :], y[:, t, 0:BLOCK], ACT.Tanh).then_inc(tanh_ready, 1)
                elif what == "scores":
                    act.wait_ge(masked, n + 1)
                    for t, (a, b) in enumerate(((0, P), (P, 3 * P))):
                        last = nc.scalar.activation(probs[:, n % 2, a:b], probs[:, n % 2, a:b], ACT.Exp,
                                                    scale=-1.0, bias=least[:, n, t:t + 1],
                                                    accum_out=den[:, n, t:t + 1])
                    last.then_inc(probs_ready, 1)
                elif what == "transpose":
                    act.wait_ge(probs_turned, n + 1)
                    if n >= 2:
                        act.wait_ge(values_done, n // 2)
                    nc.scalar.copy(probsT[:, n % 2, :], turn_bank[:, 0:3 * P]).then_inc(probsT_ready, 1)
                elif what == "y_pair":
                    act.wait_ge(y_turned, n + 1)
                    chunk, bank = y_place(n)
                    nc.scalar.copy(yT_hi[:, chunk:chunk + 2, :],
                                   bank[:].rearrange("p (a b) -> p a b", b=SEQ)).then_inc(y_hi, 1)
                elif what == "ws":
                    act.wait_ge(ws_turned, 1)
                    nc.scalar.copy(wsT, turn_bank[:].rearrange("p (a b) -> p a b", b=P)).then_inc(wsT_ready, 1)
                elif what == "residual":
                    act.wait_ge(added, 2 * n + step[2] + 1)
                    act.wait_ge(squares, 2 * n + step[2] + 3)
                    square_sum(n + 2, step[2])
                elif what == "hidden":
                    hidden_high(n)
                elif what == "scale" and n >= 2:
                    act.wait_ge(rstd_ready, n + 3)
                    act.wait_ge(with_gain, n - 1)
                    cols = hn[:, n % TILES, BLOCK:D]
                    nc.scalar.mul(cols, cols, rstd[:, n + 2:n + 3]).then_inc(final_act, 1)

        @block.vector
        def _(dve):
            def chain(instruction, semaphore, value):
                instruction.then_inc(semaphore, 1)
                dve.wait_ge(semaphore, value)

            def windows():
                dve.wait_ge(iota_ready, 2)
                nc.vector.tensor_scalar(rel4, rel_i, 3, None, ALU.bitwise_and)
                chain(nc.vector.tensor_scalar(rel16, rel_i, 15, None, ALU.bitwise_and), mask_count, 1)
                nc.vector.tensor_scalar(part_a, rel4, 0.0, None, ALU.is_equal)
                chain(nc.vector.tensor_scalar(part_b, rel16, 0.0, None, ALU.is_equal), mask_count, 2)
                chain(nc.vector.tensor_tensor(n_held, part_a, part_b, ALU.add), mask_count, 3)
                chain(nc.vector.tensor_tensor(n_held, n_held, in_window, ALU.add), mask_count, 4)
                nc.vector.tensor_scalar(part_a, n_held, 2.0, math.log(2.0) / SCALE, ALU.is_equal, ALU.mult)
                nc.vector.tensor_scalar(part_b, n_held, 3.0, math.log(3.0) / SCALE, ALU.is_equal, ALU.mult)
                chain(nc.vector.tensor_scalar(mask_odd[:], n_held, 0.5, MASKED, ALU.is_lt, ALU.mult), mask_count, 5)
                chain(nc.vector.tensor_tensor(mask_odd[:], mask_odd[:], part_a, ALU.add), mask_count, 6)
                nc.vector.tensor_tensor(mask_odd[:], mask_odd[:], part_b, ALU.add).then_inc(mask_built, 1)

            def scale_tile(n, times):
                t = n % TILES
                source = h
                if n >= 2 * TILES:
                    source = hn
                    dve.wait_ge(final_gain_loaded, 16)
                    for c in range(2):
                        cols = slice(c * BLOCK, (c + 1) * BLOCK)
                        last = nc.vector.tensor_tensor(hn[:, t, cols], h[:, t, cols], gain[:, cols], ALU.mult)
                    last.then_inc(with_gain, 1)
                    dve.wait_ge(with_gain, t + 1)
                dve.wait_ge(rstd_ready, n + 1)
                for c in range(times):
                    cols = slice(c * BLOCK, (c + 1) * BLOCK)
                    nc.vector.tensor_scalar(hn[:, t, cols], source[:, t, cols], rstd[:, n:n + 1], None,
                                            ALU.mult).then_inc(scaled, 1)

            def hidden_low(n):
                t = n % TILES
                for i, bank in enumerate((score_banks, (turn_bank, value_bank))[t]):
                    dve.wait_ge(hidden_hi, 2 * n + i + 1)
                    for c in range(4):
                        gain_col = CHUNKS * (n // TILES) + 4 * i + c
                        place = (slice(None), 4 * i + c, slice(t * P, (t + 1) * P))
                        last = nc.vector.scalar_tensor_tensor(
                            out=hnT_lo[place], in0=bank[:, c * P:(c + 1) * P], scalar=gain_of[:, gain_col:gain_col + 1],
                            in1=hnT_hi[place].bitcast(fp32), op0=ALU.mult, op1=ALU.subtract)
                    last.then_inc(hidden_ready, 1)

            dve.wait_ge(x_loaded[0], 16)
            nc.vector.tensor_tensor_reduce(out=hn[:, 0, BLOCK:D], in0=h[:, 0, BLOCK:D], in1=h[:, 0, BLOCK:D],
                                           scale=1.0 / D, scalar=0.0, op0=ALU.mult, op1=ALU.add,
                                           accum_out=sumsq[:, 0, 1:2]).then_inc(squares_dve, 1)
            dve.wait_ge(rstd_ready, 1)
            for c in range(2):
                cols = slice(c * BLOCK, (c + 1) * BLOCK)
                nc.vector.tensor_scalar(hn[:, 0, cols], h[:, 0, cols], rstd[:, 0:1], None,
                                        ALU.mult).then_inc(scaled, 1)

            for step in order:
                what, n = step[0], step[1]
                if what == "rest":
                    half, quarter = n // 2, n % 2
                    dve.wait_ge(hi_ready, n + 1)
                    part = slice(2 * quarter, 2 * quarter + 2)
                    nc.vector.tensor_tensor(w_lo[:, n % SPLIT_SLOTS, :, :], w_raw[:, half % RAW_SLOTS, part, :],
                                            w_hi[:, n % SPLIT_SLOTS, :, :].bitcast(fp32),
                                            ALU.subtract).then_inc(lo_ready, 1)
                elif what == "norm":
                    dve.wait_ge(x_loaded[1], 16)
                    dve.wait_ge(rstd_ready, 2)
                    for c in range(2):
                        cols = slice(c * BLOCK, (c + 1) * BLOCK)
                        nc.vector.tensor_scalar(hn[:, 1, cols], h[:, 1, cols], rstd[:, 1:2], None,
                                                ALU.mult).then_inc(first_scaled, 1)
                elif what == "again" and KEYS_AGAIN_BY[step[2]] == "dve":
                    keys_again(dve, nc.vector.tensor_copy, n, step[2])
                elif what == "evacuate" and GROUPS_OF_BANKS[n][0] in SPLIT_KINDS:
                    heads_set = set_of_heads(n)
                    banks_before = 2 * count_of_kind(SPLIT_KINDS, n - 1)
                    for i, bank in enumerate(pair(n)):
                        dve.wait_ge(heads_high, banks_before + i + 1)
                        for side in range(2):
                            rows, those = rows_of(side), heads_of(i, side)
                            if GROUPS_OF_BANKS[n][0] == "query":
                                high = q_stack[heads_set][rows, those, :]
                                to = q_stack[heads_set][rows_of(1 - side), those, :]
                            else:
                                high = k_twice[heads_set][rows, those, :]
                                to = k_rest[heads_set][rows, 2 * i:2 * i + 2, :]
                            last = nc.vector.tensor_tensor(to, bank[rows, :].rearrange("p (a b) -> p a b", b=SEQ),
                                                           high.bitcast(fp32), ALU.subtract)
                        last.then_inc(heads_low, 1)
                elif what == "evacuate" and GROUPS_OF_BANKS[n][0] == "gate":
                    for t, bank in enumerate(pair(n)):
                        dve.wait_ge(tanh_ready, tanh_writes_before(n) + t + 1)
                        last = nc.vector.scalar_tensor_tensor(
                            out=gate[:, GROUPS_OF_BANKS[n][1], t, :], in0=tanh[:, t, :], scalar=1.0, in1=bank[:],
                            op0=ALU.add, op1=ALU.mult)
                    last.then_inc(dve_emptied, 1)
                elif what == "gelu_inner":
                    first = TILES * sum(k == "gelu" for k, _ in GROUPS_OF_BANKS[:n])
                    for t, bank in enumerate(pair(n)):
                        dve.wait_ge(squared, first + t + 1)
                        nc.vector.scalar_tensor_tensor(out=y[:, t, 0:BLOCK], in0=y[:, t, 0:BLOCK], scalar=GELU_C,
                                                       in1=bank[:], op0=ALU.add, op1=ALU.mult
                                                       ).then_inc(inner_ready, 1)
                elif what == "gelu_outer":
                    place = GROUPS_OF_BANKS[n][1] * BLOCK
                    if place == 0:
                        dve.wait_ge(mix_done, TILES)
                    for t, bank in enumerate(pair(n)):
                        dve.wait_ge(tanh_ready, tanh_writes_before(n) + t + 1)
                        last = nc.vector.scalar_tensor_tensor(
                            out=hn[:, t, place:place + BLOCK], in0=tanh[:, t, :], scalar=1.0, in1=bank[:],
                            op0=ALU.add, op1=ALU.mult)
                    last.then_inc(dve_emptied, 1)
                elif what == "layer_norm":
                    vt = hn[:, n, BLOCK:D]
                    dve.wait_ge(dve_emptied, dve_emptied_before(4) + 1)
                    chain(nc.vector.bn_stats(moments[:, n, :], vt), stats, n + 1)
                    nc.vector.bn_aggr(meanvar[:, n, :], moments[:, n, :]).then_inc(stats2, 1)
                    dve.wait_ge(stats2, n + 1)
                    dve.wait_ge(ln_loaded, 32)
                    nc.vector.scalar_tensor_tensor(out=vt, in0=vt, scalar=meanvar[:, n, 0:1], in1=ln_g,
                                                   op0=ALU.subtract, op1=ALU.mult).then_inc(centred, 1)
                    dve.wait_ge(centred, n + 1)
                    dve.wait_ge(ln_plus, 2 * n + 2)
                    nc.vector.scalar_tensor_tensor(out=vt, in0=vt, scalar=rstd[:, 6 + n:7 + n], in1=ln_b,
                                                   op0=ALU.mult, op1=ALU.add).then_inc(v_normed, 1)
                elif what == "mix_u":
                    dve.wait_ge(mix_done, n + 1)
                    dve.wait_ge(bias_loaded, 16)
                    dve.wait_ge(dve_emptied, dve_emptied_before(6) + 1)
                    for g in range(GROUPS):
                        cols = slice(g * P, (g + 1) * P)
                        last = nc.vector.scalar_tensor_tensor(
                            out=y[:, n, cols], in0=score_banks[n][:, cols], scalar=bias_s[:, g:g + 1],
                            in1=hn[:, n, cols], op0=ALU.add, op1=ALU.mult)
                    last.then_inc(mixed, 1)
                elif what == "gating":
                    for t in range(TILES):
                        if n == 1:
                            dve.wait_ge(mixed, TILES)
                            dve.wait_ge(dve_emptied, dve_emptied_before(7) + 1)
                            last = nc.vector.scalar_tensor_tensor(
                                out=y[:, t, 0:BLOCK], in0=y[:, t, 0:BLOCK], scalar=0.25, in1=gate[:, 0, t, :],
                                op0=ALU.mult, op1=ALU.mult)
                        else:
                            c = {0: 1, 2: 0, 3: 1}[n]
                            dve.wait_ge(attended, {0: EVEN_HEADS, 2: EVEN_HEADS + 8, 3: N_HEADS}[n] // 2)
                            dve.wait_ge(dve_emptied, dve_emptied_before({0: 5, 2: 16, 3: 17}[n]) + 1)
                            cols = slice((c if n else 1) * BLOCK, (c + 1 if n else 2) * BLOCK)
                            last = nc.vector.tensor_tensor(y[:, t, cols], y[:, t, cols], gate[:, c, t, :], ALU.mult)
                    last.then_inc(gated, 1)
                elif what == "scores":
                    mask = mask_even if n < EVEN_HEADS else mask_odd
                    dve.wait_ge(scores_done, n + 1)
                    if n == 0:
                        dve.wait_ge(const_pool, 2)
                    if n == EVEN_HEADS:
                        dve.wait_ge(mask_built, 2)
                    if n >= 2:
                        dve.wait_ge(probs_turned, n - 1)
                    for t, (a, b) in enumerate(((0, P), (P, 3 * P))):
                        last = nc.vector.tensor_tensor_reduce(
                            out=probs[:, n % 2, a:b], in0=score_banks[n % 2][:, a:b], in1=mask[:, 2 * P - (b - a):],
                            scale=-SCALE, scalar=3e38, op0=ALU.add, op1=ALU.min, accum_out=least[:, n, t:t + 1])
                    last.then_inc(masked, 1)
                elif what == "values":
                    pair_of = slice(2 * n, 2 * n + 2)
                    dve.wait_ge(values_done, n + 1)
                    chain(nc.vector.reciprocal(rden[:, pair_of, :], den[:, pair_of, :]), inverted, n + 1)
                    column = value_column(2 * n) + (BLOCK if n < EVEN_HEADS // 2 else 0)
                    nc.vector.tensor_tensor(
                        y[:, :, column:column + 2 * HEAD].rearrange("p t (a d) -> p a t d", a=2),
                        value_bank[:, 0:4 * HEAD].rearrange("p (a t d) -> p a t d", a=2, t=TILES),
                        rden[:, pair_of, :].unsqueeze(3).to_broadcast([P, 2, TILES, HEAD]),
                        ALU.mult).then_inc(attended, 1)
                elif what == "y_pair":
                    chunk, bank = y_place(n)
                    dve.wait_ge(y_hi, n + 1)
                    nc.vector.tensor_tensor(yT_lo[:, chunk:chunk + 2, :], bank[:].rearrange("p (a b) -> p a b", b=SEQ),
                                            yT_hi[:, chunk:chunk + 2, :].bitcast(fp32), ALU.subtract).then_inc(y_lo, 1)
                elif what == "residual":
                    layer, t, c = n // TILES, n % TILES, step[2]
                    group = (8, 18)[layer] + t
                    dve.wait_ge(products_done, LAST_ITEM_OF_GROUP[group] + 1 - 2 * (1 - c))
                    cols = slice(c * BLOCK, (c + 1) * BLOCK)
                    nc.vector.tensor_tensor(h[:, t, cols], h[:, t, cols], pair(group)[c][:],
                                            ALU.add).then_inc(added, 1)
                elif what == "windows":
                    windows()
                elif what == "scale":
                    dve.wait_ge(added, 2 * n + 2)
                    scale_tile(2 + n, 2 if n < TILES else 1)
                elif what == "hidden":
                    hidden_low(n)

        @block.tensor
        def _(pe):
            def turn(to, of):
                return nc.tensor.matmul(to, of, ident[:], is_transpose=True, start=True, stop=True)

            def hidden_turn(n):
                t = n % TILES
                for i, bank in enumerate((score_banks, (turn_bank, value_bank))[t]):
                    if n == 1:
                        pe.wait_ge(first_scaled, i + 1)
                    else:
                        pe.wait_ge(scaled, 2 * (n - 1 if n else 0) + i + 1)
                    for c in range(4):
                        last = turn(bank[:, c * P:(c + 1) * P], hn[:, t, (4 * i + c) * P:(4 * i + c + 1) * P])
                    last.then_inc(hidden_turned, 1)

            def keep_warm(times):
                for _ in range(times):
                    nc.tensor.matmul(value_bank[:, 0:P], ident[:], ident[:], start=True, stop=True)

            pe.wait_ge(const_pool, 2)
            keep_warm(WARM[0])
            pe.wait_ge(gains_loaded, 16)
            nc.tensor.matmul(turn_bank[:, 0:2 * CHUNKS], gain_rows[:], ident[0:2 * CHUNKS, 0:2 * CHUNKS],
                             is_transpose=True, start=True, stop=True).then_inc(gains_turned, 1)
            keep_warm(WARM[1])
            started = set()
            pairs_valued = pairs_turned = 0
            for step in order:
                what, n = step[0], step[1]
                if what == "product":
                    half_item = step[2]
                    group, half, quarter, side = ITEMS[n]
                    kind, place = GROUPS_OF_BANKS[group]
                    matrix, chunk0, _ = HALVES[half]
                    if half_item == 0:
                        if kind == "value_half":
                            pe.wait_ge(hidden_ready, 2 * place + (chunk0 > 0) + 1)
                        pe.wait_ge(lo_ready, 2 * half + quarter + 1)
                        if group >= 2 and group not in started:
                            wait_emptied(pe, group - 2)
                        started.add(group)
                        if kind == "residual":
                            layer = 0 if matrix == "even_out" else 1
                            pairs = [y_place(i)[0] for i in range(HALF_CHUNKS * layer, HALF_CHUNKS * (layer + 1))]
                            pe.wait_ge(y_lo, HALF_CHUNKS * layer + pairs.index(chunk0 + 2 * quarter) + 1)
                        if kind == "value_tile":
                            pe.wait_ge(hidden_ready, 2 * (TILES + place) + (chunk0 > 0) + 1)
                    hi, lo = (yT_hi, yT_lo) if kind == "residual" else (hnT_hi, hnT_lo)
                    r = 2 * quarter + half_item
                    chunk = chunk0 + r
                    slot = (2 * half + quarter) % SPLIT_SLOTS
                    begins = chunk == (HALF_CHUNKS if matrix == "even_out" else 0)
                    ends = chunk == (HALF_CHUNKS - 1 if matrix == "even_out" else CHUNKS - 1)
                    if kind in ("query", "key"):
                        for c in range(4):
                            to = pair(group)[c // 2][:, (c % 2) * SEQ:(c % 2 + 1) * SEQ]
                            cols = slice(c * P, (c + 1) * P)
                            wh, wl = w_hi[:, slot, half_item, cols], w_lo[:, slot, half_item, cols]
                            nc.tensor.matmul(to, wh, hi[:, chunk, :], start=begins and c % 2 == 0, stop=False,
                                             skip_group_check=True)
                            nc.tensor.matmul(to, wh, lo[:, chunk, :], start=False, stop=False,
                                             skip_group_check=True)
                            last = nc.tensor.matmul(to, wl, hi[:, chunk, :], start=False, stop=ends,
                                                    skip_group_check=True)
                    else:
                        if side is None:
                            targets = [(t, pair(group)[t]) for t in range(TILES)]
                        else:
                            targets = [(place, pair(group)[side])]
                        for t, to in targets:
                            rows = slice(t * P, (t + 1) * P)
                            xh, xl = hi[:, chunk, rows], lo[:, chunk, rows]
                            nc.tensor.matmul(to[:], xh, w_hi[:, slot, half_item, :], start=begins, stop=False)
                            nc.tensor.matmul(to[:], xl, w_hi[:, slot, half_item, :], start=False, stop=False)
                            last = nc.tensor.matmul(to[:], xh, w_lo[:, slot, half_item, :], start=False, stop=ends)
                    if half_item == 1:
                        last.then_inc(products_done, 1)
                elif what == "scores":
                    heads_set, i = divmod(n, HEADS_OF_SET)
                    if n in (0, EVEN_HEADS):
                        pe.wait_ge(act_emptied, TILES if n == 0 else 2 * TILES)
                    if i % 4 == 0:
                        pe.wait_ge(keys_twice[i // 4], heads_set + 1)
                        pe.wait_ge(heads_low, 4 * heads_set + 2 + i // 4 + 1)
                    if n >= 2:
                        pe.wait_ge(masked, n - 1)
                    rows = rows_of(i % 2)
                    q, k = q_stack[heads_set], k_twice[heads_set]
                    k_lo = k_rest[heads_set]
                    bank = score_banks[n % 2]
                    for t, (a, b) in enumerate(((0, P), (P, 3 * P))):
                        queries, keys = slice(t * P, (t + 1) * P), slice(0, b - a)
                        nc.tensor.matmul(bank[:, a:b], q[:, i, queries], k[:, i, keys], start=True, stop=False)
                        last = nc.tensor.matmul(bank[:, a:b], q[rows, i, queries], k_lo[rows, i // 2, keys],
                                                start=False, stop=True)
                    last.then_inc(scores_done, 1)
                elif what == "transpose":
                    pe.wait_ge(probs_ready, n + 1)
                    if n >= 1:
                        pe.wait_ge(probsT_ready, n)
                    for i in range(3):
                        last = turn(turn_bank[:, i * P:(i + 1) * P], probs[:, n % 2, i * P:(i + 1) * P])
                    last.then_inc(probs_turned, 1)
                elif what == "values":
                    pe.wait_ge(probsT_ready, 2 * n + 2)
                    if n >= 1:
                        pe.wait_ge(attended, n)
                    if pairs_turned:
                        pe.wait_ge(y_lo, pairs_turned)
                    pairs_valued = n + 1
                    for a in range(2):
                        column = value_column(2 * n + a)
                        pT = probsT[:, a, :]
                        v0, v1 = v[:, 0, column:column + HEAD], v[:, 1, column:column + HEAD]
                        first, second = (value_bank[:, (2 * a + t) * HEAD:(2 * a + t + 1) * HEAD] for t in range(2))
                        nc.tensor.matmul(first, pT[:, 0:P], v0, start=True, stop=True)
                        nc.tensor.matmul(second, pT[:, P:2 * P], v0, start=True, stop=False)
                        last = nc.tensor.matmul(second, pT[:, 2 * P:3 * P], v1, start=False, stop=True)
                    last.then_inc(values_done, 1)
                elif what == "mix":
                    pe.wait_ge(wsT_ready, 1)
                    pe.wait_ge(v_normed, n + 1)
                    pe.wait_ge(masked, EVEN_HEADS)
                    for g in range(GROUPS):
                        cols = slice(BLOCK + g * P, BLOCK + (g + 1) * P)
                        last = nc.tensor.matmul(score_banks[n][:, g * P:(g + 1) * P], wsT[:, g, :], hn[:, n, cols],
                                                start=True, stop=True)
                    last.then_inc(mix_done, 1)
                elif what == "y_pair":
                    chunk, bank = y_place(n)
                    pe.wait_ge(gated, n // 2 + 1)
                    same_bank = [i for i in range(n) if y_place(i)[1] is bank]
                    if same_bank:
                        pe.wait_ge(y_lo, same_bank[-1] + 1)
                    if bank is value_bank:
                        pe.wait_ge(attended, pairs_valued)
                        pairs_turned = n + 1
                    else:
                        pe.wait_ge(probsT_ready, EVEN_HEADS if n < HALF_CHUNKS else N_HEADS)
                    for c in range(2):
                        for t in range(TILES):
                            last = turn(bank[:, (2 * c + t) * P:(2 * c + t + 1) * P],
                                        y[:, t, (chunk + c) * P:(chunk + c + 1) * P])
                    last.then_inc(y_turned, 1)
                elif what == "ws":
                    pe.wait_ge(ws_masked, 1)
                    for g in range(GROUPS):
                        last = turn(turn_bank[:, g * P:(g + 1) * P], ws[:, g, :])
                    last.then_inc(ws_turned, 1)
                elif what == "hidden":
                    if n == 2:
                        pe.wait_ge(mixed, TILES)
                    hidden_turn(n)
                    if n == 0:
                        keep_warm(WARM[2])


_NAMES = ("x", "norm_g", "final_norm_g", "ab_w_in", "ab_w_out", "gmlp_ln_g", "gmlp_ln_b", "gmlp_w_s", "gmlp_b_s",
          "c_w_in", "c_w_out")


def kernel(**inputs):
    import numpy as np
    import concourse.bacc as bacc
    from concourse.bass_utils import run_bass_kernel_spmd

    nc = bacc.Bacc("TRN2", target_bir_lowering=False, num_devices=1)
    arrays, args = {}, []
    for name in _NAMES:
        a = np.ascontiguousarray(inputs[name])
        arrays[f"in_{name}"] = a
        args.append(nc.dram_tensor(f"in_{name}", a.shape, mybir.dt.from_np(a.dtype), kind="ExternalInput").ap())
    out = nc.dram_tensor("out_0", (1, SEQ, D), mybir.dt.float32, kind="ExternalOutput").ap()
    build(nc, *args, out)
    result = run_bass_kernel_spmd(nc, [arrays], core_ids=[0])
    return result.results[0]["out_0"]
```
